# Optimizing a Trainium2 kernel written in Bass

```python
import math
import jax
import jax.numpy as jnp
from jax import lax
import numpy as np

D_MODEL = 1024
BATCH = 1
SEQ = 1024
DEPTH = 1
DEC_BATCH = 8
DEC_SEQ = 4
PAST_LEN = 8192
PAGE_SIZE = 128

HEAD_DIM = 64
H_A = D_MODEL // 2 // HEAD_DIM
H_B = D_MODEL // 2 // HEAD_DIM
G_B = 2
R_B = H_B // G_B
H_TOTAL = H_A + H_B
D_MIX = H_TOTAL * HEAD_DIM
DILATED_PATTERNS = ((128, 1), (512, 4), (2048, 16))
A_WINDOW = 2048
BAND_BLOCK = 128
NSA_BLOCK = 64
NSA_TOPN = 16
NSA_WINDOW = 512
SEL_QCHUNK = 32
FORCE_SCORE = 1e4
N_BUCKETS = 32
BUCKET_MAX_DIST = 2048
D_FF = 2816
CONV_W = 3
EPS = 1e-6
NEG = -1e30
ATT_SCALE = HEAD_DIM ** -0.5
IN_SPLITS = (H_A * HEAD_DIM, H_A * HEAD_DIM, H_A * HEAD_DIM, H_B * HEAD_DIM) + (G_B * HEAD_DIM,) * 6 + (3 * H_B,)
N_IN = sum(IN_SPLITS)

kernel_name = 'hybrid_dilated_nsa_convffn_step'

def _rms_norm(x, g):
    xf = x.astype(jnp.float32)
    y = xf * lax.rsqrt(jnp.mean(xf * xf, axis=-1, keepdims=True) + EPS)
    return (y * g.astype(jnp.float32)).astype(x.dtype)

def _t5_bucket(dist):
    dist = jnp.maximum(dist, 0)
    max_exact = N_BUCKETS // 2
    d = jnp.maximum(dist, 1).astype(jnp.float32)
    large = max_exact + (jnp.log(d / max_exact) / math.log(BUCKET_MAX_DIST / max_exact)
                         * (N_BUCKETS - max_exact)).astype(jnp.int32)
    return jnp.where(dist < max_exact, dist, jnp.minimum(large, N_BUCKETS - 1))

def _masked_softmax(logits, mask):
    logits = jnp.where(mask, logits, NEG)
    m = jnp.max(logits, axis=-1, keepdims=True)
    p = jnp.where(mask, jnp.exp(logits - m), 0.0)
    s = jnp.sum(p, axis=-1, keepdims=True)
    s_safe = jnp.where(s > 0, s, 1.0)
    return p / s_safe, (m + jnp.log(s_safe))[..., 0]

def _banded_attention(q, k, v, window, dist_scale, bias_tab):
    n, length, g, r, dh = q.shape
    blk = BAND_BLOCK
    nb = -(-length // blk)
    pad = nb * blk - length
    n_prev = -(-window // blk)
    qb = jnp.pad(q, ((0, 0), (0, pad), (0, 0), (0, 0), (0, 0))).reshape(n, nb, blk, g, r, dh)

    def key_blocks(x):
        xp = jnp.pad(x, ((0, 0), (n_prev * blk, pad), (0, 0), (0, 0))).reshape(n, nb + n_prev, blk, g, dh)
        return jnp.concatenate([xp[:, s:s + nb] for s in range(n_prev + 1)], axis=2)

    kb, vb = key_blocks(k), key_blocks(v)
    qi = jnp.arange(blk)[:, None]
    kj = jnp.arange((n_prev + 1) * blk)[None, :]
    rel = n_prev * blk + qi - kj
    key_idx = jnp.arange(nb)[:, None, None] * blk + kj[None] - n_prev * blk
    mask = (rel >= 0) & (rel <= window) & (key_idx >= 0)
    bias = jnp.transpose(bias_tab[_t5_bucket(rel * dist_scale)], (2, 3, 0, 1))
    logits = jnp.einsum('nbqgrd,nbkgd->nbgrqk', qb, kb, preferred_element_type=jnp.float32) * ATT_SCALE + bias
    probs, lse = _masked_softmax(logits, mask[None, :, None, None])
    out = jnp.einsum('nbgrqk,nbkgd->nbqgrd', probs, vb.astype(jnp.float32))
    out = out.reshape(n, nb * blk, g, r, dh)[:, :length]
    lse = jnp.transpose(lse, (0, 1, 4, 2, 3)).reshape(n, nb * blk, g, r)[:, :length]
    return out, lse

def _merge_by_denominator(outs, lses):
    w = jax.nn.softmax(jnp.stack(lses, axis=0), axis=0)
    return jnp.sum(w[..., None] * jnp.stack(outs, axis=0), axis=0)

def _dilated_prompt(q, k, v, bias_a):
    b, s = q.shape[:2]
    outs, lses = [], []
    for window, dil in DILATED_PATTERNS:
        ln = s // dil

        def by_stride(x):
            return jnp.swapaxes(x.reshape(b, ln, dil, *x.shape[2:]), 1, 2).reshape(b * dil, ln, *x.shape[2:])

        o, lse = _banded_attention(by_stride(q)[..., None, :], by_stride(k), by_stride(v),
                                   window // dil, dil, bias_a)
        outs.append(jnp.swapaxes(o.reshape(b, dil, ln, H_A, HEAD_DIM), 1, 2).reshape(b, s, H_A, HEAD_DIM))
        lses.append(jnp.swapaxes(lse.reshape(b, dil, ln, H_A), 1, 2).reshape(b, s, H_A))
    return _merge_by_denominator(outs, lses)

def _dilated_sample(q, k_cat, v_cat, buf_len, bias_a):
    t = q.shape[1]
    outs, lses = [], []
    for window, dil in DILATED_PATTERNS:
        j = jnp.arange(window // dil + 1)
        idx = buf_len + jnp.arange(t)[:, None] - j[None, :] * dil
        valid = idx >= 0
        idx = jnp.maximum(idx, 0)
        kg, vg = k_cat[:, idx], v_cat[:, idx]
        bias = bias_a[_t5_bucket(j * dil), :, 0].T
        logits = jnp.einsum('bthd,btnhd->bthn', q, kg, preferred_element_type=jnp.float32) * ATT_SCALE + bias
        probs, lse = _masked_softmax(logits, valid[None, :, None, :])
        outs.append(jnp.einsum('bthn,btnhd->bthd', probs, vg.astype(jnp.float32)))
        lses.append(lse)
    return _merge_by_denominator(outs, lses)

def _compress(x, pe, w1, w2):
    n, n_tok = x.shape[:2]
    nbc = -(-n_tok // NSA_BLOCK)
    x = jnp.pad(x, ((0, 0), (0, nbc * NSA_BLOCK - n_tok), (0, 0), (0, 0)))
    xb = x.reshape(n, nbc, NSA_BLOCK, G_B, HEAD_DIM) + pe[None, None, :, None, :]
    xb = jnp.transpose(xb, (0, 1, 3, 2, 4)).reshape(n, nbc, G_B, NSA_BLOCK * HEAD_DIM)
    return jax.nn.gelu(xb @ w1) @ w2

def _nsa_compressed(q, kc, vc, q_pos, bias_b):
    nbc = kc.shape[1]
    blk_end = (jnp.arange(nbc) + 1) * NSA_BLOCK - 1
    rel = q_pos[:, None] - blk_end[None, :]
    bias = jnp.transpose(bias_b[_t5_bucket(rel)], (0, 2, 3, 1))
    logits = jnp.einsum('ntgrd,nkgd->ntgrk', q, kc, preferred_element_type=jnp.float32) * ATT_SCALE + bias
    probs, _ = _masked_softmax(logits, (rel >= 0)[None, :, None, None, :])
    out = jnp.einsum('ntgrk,nkgd->ntgrd', probs, vc.astype(jnp.float32))
    return out, jnp.sum(probs, axis=3)

def _nsa_select(p_slc, q_pos):
    nbc = p_slc.shape[-1]
    blk = jnp.arange(nbc)[None, :]
    cur = (q_pos // NSA_BLOCK)[:, None]
    forced = (blk == 0) | (blk == cur) | (blk == cur - 1)
    started = blk <= cur
    score = jnp.where(forced[None, :, None, :], FORCE_SCORE, p_slc)
    score = jnp.where(started[None, :, None, :], score, -1.0)
    top_s, top_i = lax.top_k(score, min(NSA_TOPN, nbc))
    return top_i, top_s >= 0.0

def _nsa_selected_core(q, kg, vg, key_pos, key_ok, q_pos, bias_b):
    rel = q_pos[None, :, None, None] - key_pos
    g_idx = jnp.arange(G_B)[None, None, :, None]
    bias = jnp.swapaxes(bias_b[_t5_bucket(rel), g_idx], -1, -2)
    logits = jnp.einsum('ntgrd,ntgkd->ntgrk', q, kg, preferred_element_type=jnp.float32) * ATT_SCALE + bias
    probs, _ = _masked_softmax(logits, (key_ok & (rel >= 0))[:, :, :, None, :])
    return jnp.einsum('ntgrk,ntgkd->ntgrd', probs, vg.astype(jnp.float32))

def _nsa_selected_prompt(q, ks, vs, top_i, top_ok, q_pos, bias_b):
    b, s = q.shape[:2]
    nbc = s // NSA_BLOCK
    n_sel = top_i.shape[-1]
    kb = jnp.transpose(ks.reshape(b, nbc, NSA_BLOCK, G_B, HEAD_DIM), (0, 3, 1, 2, 4))
    vb = jnp.transpose(vs.reshape(b, nbc, NSA_BLOCK, G_B, HEAD_DIM), (0, 3, 1, 2, 4))
    b_idx = jnp.arange(b)[:, None, None, None]
    g_idx = jnp.arange(G_B)[None, None, :, None]
    offs = jnp.arange(NSA_BLOCK)
    nc = s // SEL_QCHUNK

    def chunks(x):
        return jnp.swapaxes(x.reshape(b, nc, SEL_QCHUNK, *x.shape[2:]), 0, 1)

    def one_chunk(args):
        qc, ic, okc, pc = args
        kg = kb[b_idx, g_idx, ic].reshape(b, SEL_QCHUNK, G_B, n_sel * NSA_BLOCK, HEAD_DIM)
        vg = vb[b_idx, g_idx, ic].reshape(b, SEL_QCHUNK, G_B, n_sel * NSA_BLOCK, HEAD_DIM)
        key_pos = (ic[..., None] * NSA_BLOCK + offs).reshape(b, SEL_QCHUNK, G_B, n_sel * NSA_BLOCK)
        key_ok = jnp.broadcast_to(okc[..., None], (b, SEL_QCHUNK, G_B, n_sel, NSA_BLOCK)).reshape(key_pos.shape)
        return _nsa_selected_core(qc, kg, vg, key_pos, key_ok, pc, bias_b)

    out = lax.map(one_chunk, (chunks(q), chunks(top_i), chunks(top_ok), q_pos.reshape(nc, SEL_QCHUNK)))
    return jnp.swapaxes(out, 0, 1).reshape(b, s, G_B, R_B, HEAD_DIM)

def _nsa_selected_sample(q, ks_new, vs_new, pool_k, pool_v, page_table, top_i, top_ok, q_pos, bias_b):
    db, t = q.shape[:2]
    n_sel = top_i.shape[-1]
    pos = top_i[..., None] * NSA_BLOCK + jnp.arange(NSA_BLOCK)
    b_idx = jnp.arange(db)[:, None, None, None, None]
    g_idx = jnp.arange(G_B)[None, None, :, None, None]
    in_past = (pos < PAST_LEN)[..., None]
    pp = jnp.minimum(pos, PAST_LEN - 1)
    phys = page_table[b_idx, pp // PAGE_SIZE]
    off = pp % PAGE_SIZE
    pn = jnp.clip(pos - PAST_LEN, 0, t - 1)

    def gather(pool, new):
        rows = jnp.where(in_past, pool[phys, off, g_idx], new[b_idx, pn, g_idx])
        return rows.reshape(db, t, G_B, n_sel * NSA_BLOCK, HEAD_DIM)

    key_pos = pos.reshape(db, t, G_B, n_sel * NSA_BLOCK)
    key_ok = jnp.broadcast_to(top_ok[..., None], pos.shape).reshape(key_pos.shape)
    return _nsa_selected_core(q, gather(pool_k, ks_new), gather(pool_v, vs_new), key_pos, key_ok, q_pos, bias_b)

def _nsa_window_sample(q, kw_cat, vw_cat, q_pos, bias_b):
    t = q.shape[1]
    n_keys = kw_cat.shape[1]
    key_pos = PAST_LEN + t - n_keys + jnp.arange(n_keys)
    rel = q_pos[:, None] - key_pos[None, :]
    bias = jnp.transpose(bias_b[_t5_bucket(rel)], (0, 2, 3, 1))
    logits = jnp.einsum('ntgrd,nkgd->ntgrk', q, kw_cat, preferred_element_type=jnp.float32) * ATT_SCALE + bias
    probs, _ = _masked_softmax(logits, ((rel >= 0) & (rel <= NSA_WINDOW))[None, :, None, None, :])
    return jnp.einsum('ntgrk,nkgd->ntgrd', probs, vw_cat.astype(jnp.float32))

def _mix_inputs(x, norm_attn, w_in):
    n, t = x.shape[:2]
    y = _rms_norm(x, norm_attn) @ w_in
    idx = np.cumsum(IN_SPLITS)[:-1].tolist()
    qa, ka, va, qb, kc, vc, ks, vs, kw, vw, gates = jnp.split(y, idx, axis=-1)
    heads_a = lambda z: z.reshape(n, t, H_A, HEAD_DIM)
    kv_b = lambda z: z.reshape(n, t, G_B, HEAD_DIM)
    gates = jax.nn.sigmoid(gates.astype(jnp.float32)).reshape(n, t, G_B, R_B, 3)
    return (heads_a(qa), heads_a(ka), heads_a(va), qb.reshape(n, t, G_B, R_B, HEAD_DIM),
            kv_b(kc), kv_b(vc), kv_b(ks), kv_b(vs), kv_b(kw), kv_b(vw), gates)

def _gate_branches(gates, o_cmp, o_slc, o_win):
    return gates[..., 0:1] * o_cmp + gates[..., 1:2] * o_slc + gates[..., 2:3] * o_win

def _out_and_ffn(x, o_a, o_b, w_out, norm_ffn, w_up, conv_w, conv_b, w_down, conv_prev):
    n, t = x.shape[:2]
    mix = jnp.concatenate([o_a.reshape(n, t, H_A * HEAD_DIM), o_b.reshape(n, t, H_B * HEAD_DIM)], axis=-1)
    x = x + mix.astype(x.dtype) @ w_out
    u = _rms_norm(x, norm_ffn) @ w_up
    u_ext = jnp.concatenate([conv_prev.astype(u.dtype), u], axis=1)
    c = conv_b
    for j in range(CONV_W):
        c = c + conv_w[j] * u_ext[:, j:j + t]
    gate, val = jnp.split(c, 2, axis=-1)
    x = x + (jax.nn.silu(gate) * val) @ w_down
    return x, u_ext[:, -(CONV_W - 1):]

def setup_inputs(seed: int = 0) -> dict:
    key = jax.random.key(seed)
    ks = jax.random.split(key, 32)
    f32 = jnp.float32

    def nrm(k, shape, scale=1.0):
        return scale * jax.random.normal(k, shape, f32)

    def gain(k, shape):
        return 1.0 + 0.02 * jax.random.normal(k, shape, f32)

    n_pages = PAST_LEN // PAGE_SIZE
    n_used = DEC_BATCH * n_pages
    n_pool = n_used + n_used // 4
    la = min(A_WINDOW, PAST_LEN)
    lw = min(NSA_WINDOW, PAST_LEN)
    pool_shape = (DEPTH, n_pool, PAGE_SIZE, G_B, HEAD_DIM)
    page_table = jax.random.permutation(ks[0], n_pool)[:n_used].reshape(DEC_BATCH, n_pages).astype(jnp.int32)
    return {
        'x_prompt': nrm(ks[1], (BATCH, SEQ, D_MODEL)),
        'x_sample': nrm(ks[2], (DEC_BATCH, DEC_SEQ, D_MODEL)),
        'cache_a_k': nrm(ks[3], (DEPTH, DEC_BATCH, la, H_A, HEAD_DIM)),
        'cache_a_v': nrm(ks[4], (DEPTH, DEC_BATCH, la, H_A, HEAD_DIM)),
        'cache_win_k': nrm(ks[5], (DEPTH, DEC_BATCH, lw, G_B, HEAD_DIM)),
        'cache_win_v': nrm(ks[6], (DEPTH, DEC_BATCH, lw, G_B, HEAD_DIM)),
        'cache_cmp_k': nrm(ks[7], pool_shape),
        'cache_cmp_v': nrm(ks[8], pool_shape),
        'cache_slc_k': nrm(ks[9], pool_shape),
        'cache_slc_v': nrm(ks[10], pool_shape),
        'state_conv': nrm(ks[11], (DEPTH, DEC_BATCH, CONV_W - 1, 2 * D_FF)),
        'page_table': page_table,
        'norm_attn': gain(ks[12], (DEPTH, D_MODEL)),
        'w_in': nrm(ks[13], (DEPTH, D_MODEL, N_IN), D_MODEL ** -0.5),
        'rel_bias': nrm(ks[14], (N_BUCKETS, H_TOTAL), 0.3),
        'pe_cmp_k': nrm(ks[15], (DEPTH, NSA_BLOCK, HEAD_DIM), 0.3),
        'w_cmp_k1': nrm(ks[16], (DEPTH, NSA_BLOCK * HEAD_DIM, HEAD_DIM), (NSA_BLOCK * HEAD_DIM) ** -0.5),
        'w_cmp_k2': nrm(ks[17], (DEPTH, HEAD_DIM, HEAD_DIM), 2.0 * HEAD_DIM ** -0.5),
        'pe_cmp_v': nrm(ks[18], (DEPTH, NSA_BLOCK, HEAD_DIM), 0.3),
        'w_cmp_v1': nrm(ks[19], (DEPTH, NSA_BLOCK * HEAD_DIM, HEAD_DIM), (NSA_BLOCK * HEAD_DIM) ** -0.5),
        'w_cmp_v2': nrm(ks[20], (DEPTH, HEAD_DIM, HEAD_DIM), 2.0 * HEAD_DIM ** -0.5),
        'w_out': nrm(ks[21], (DEPTH, D_MIX, D_MODEL), D_MIX ** -0.5),
        'norm_ffn': gain(ks[22], (DEPTH, D_MODEL)),
        'w_up': nrm(ks[23], (DEPTH, D_MODEL, 2 * D_FF), D_MODEL ** -0.5),
        'conv_w': nrm(ks[24], (DEPTH, CONV_W, 2 * D_FF), CONV_W ** -0.5),
        'conv_b': nrm(ks[25], (DEPTH, 2 * D_FF), 0.02),
        'w_down': nrm(ks[26], (DEPTH, D_FF, D_MODEL), D_FF ** -0.5),
        'norm_final': gain(ks[27], (D_MODEL,)),
    }

def reference(x_prompt, x_sample, cache_a_k, cache_a_v, cache_win_k, cache_win_v, cache_cmp_k, cache_cmp_v,
              cache_slc_k, cache_slc_v, state_conv, page_table, norm_attn, w_in, rel_bias, pe_cmp_k, w_cmp_k1,
              w_cmp_k2, pe_cmp_v, w_cmp_v1, w_cmp_v2, w_out, norm_ffn, w_up, conv_w, conv_b, w_down, norm_final):
    bias_a = rel_bias[:, :H_A].reshape(N_BUCKETS, H_A, 1)
    bias_b = rel_bias[:, H_A:].reshape(N_BUCKETS, G_B, R_B)
    b, s = x_prompt.shape[:2]
    db, t = x_sample.shape[:2]
    n_pages = page_table.shape[1]
    pos_p = jnp.arange(s)
    pos_s = PAST_LEN + jnp.arange(t)
    xp, xs = x_prompt, x_sample
    per_layer = []
    for l in range(DEPTH):
        ffn_w = (w_out[l], norm_ffn[l], w_up[l], conv_w[l], conv_b[l], w_down[l])
        cmp_k = (pe_cmp_k[l], w_cmp_k1[l], w_cmp_k2[l])
        cmp_v = (pe_cmp_v[l], w_cmp_v1[l], w_cmp_v2[l])

        qa, ka, va, qb, kc, vc, ksl, vsl, kw, vw, gates = _mix_inputs(xp, norm_attn[l], w_in[l])
        o_a = _dilated_prompt(qa, ka, va, bias_a)
        o_cmp, p_slc = _nsa_compressed(qb, _compress(kc, *cmp_k), _compress(vc, *cmp_v), pos_p, bias_b)
        top_i, top_ok = _nsa_select(p_slc, pos_p)
        o_slc = _nsa_selected_prompt(qb, ksl, vsl, top_i, top_ok, pos_p, bias_b)
        o_win, _ = _banded_attention(qb, kw, vw, NSA_WINDOW, 1, bias_b)
        o_b = _gate_branches(gates, o_cmp, o_slc, o_win)
        xp, conv_p = _out_and_ffn(xp, o_a, o_b, *ffn_w, jnp.zeros((b, CONV_W - 1, 2 * D_FF), xp.dtype))

        qa2, ka2, va2, qb2, kc2, vc2, ks2, vs2, kw2, vw2, gates2 = _mix_inputs(xs, norm_attn[l], w_in[l])
        ka_cat = jnp.concatenate([cache_a_k[l].astype(ka2.dtype), ka2], axis=1)
        va_cat = jnp.concatenate([cache_a_v[l].astype(va2.dtype), va2], axis=1)
        o_a2 = _dilated_sample(qa2, ka_cat, va_cat, cache_a_k.shape[2], bias_a)
        kc_past = cache_cmp_k[l][page_table].reshape(db, n_pages * PAGE_SIZE, G_B, HEAD_DIM)
        vc_past = cache_cmp_v[l][page_table].reshape(db, n_pages * PAGE_SIZE, G_B, HEAD_DIM)
        kcc2 = _compress(jnp.concatenate([kc_past.astype(kc2.dtype), kc2], axis=1), *cmp_k)
        vcc2 = _compress(jnp.concatenate([vc_past.astype(vc2.dtype), vc2], axis=1), *cmp_v)
        o_cmp2, p_slc2 = _nsa_compressed(qb2, kcc2, vcc2, pos_s, bias_b)
        top_i2, top_ok2 = _nsa_select(p_slc2, pos_s)
        o_slc2 = _nsa_selected_sample(qb2, ks2, vs2, cache_slc_k[l], cache_slc_v[l], page_table,
                                      top_i2, top_ok2, pos_s, bias_b)
        kw_cat = jnp.concatenate([cache_win_k[l].astype(kw2.dtype), kw2], axis=1)
        vw_cat = jnp.concatenate([cache_win_v[l].astype(vw2.dtype), vw2], axis=1)
        o_win2 = _nsa_window_sample(qb2, kw_cat, vw_cat, pos_s, bias_b)
        o_b2 = _gate_branches(gates2, o_cmp2, o_slc2, o_win2)
        xs, conv_s = _out_and_ffn(xs, o_a2, o_b2, *ffn_w, state_conv[l])

        la_p, la_s = min(A_WINDOW, s), min(A_WINDOW, ka_cat.shape[1])
        lw_p, lw_s = min(NSA_WINDOW, s), min(NSA_WINDOW, kw_cat.shape[1])
        per_layer.append((ka[:, -la_p:], ka_cat[:, -la_s:], va[:, -la_p:], va_cat[:, -la_s:],
                          kw[:, -lw_p:], kw_cat[:, -lw_s:], vw[:, -lw_p:], vw_cat[:, -lw_s:],
                          kc, kc2, vc, vc2, ksl, ks2, vsl, vs2, conv_p, conv_s))

    stacked = [jnp.stack(col, axis=0) for col in zip(*per_layer)]
    (new_a_k_p, new_a_k_s, new_a_v_p, new_a_v_s, new_win_k_p, new_win_k_s, new_win_v_p, new_win_v_s,
     new_cmp_k_p, new_cmp_k_s, new_cmp_v_p, new_cmp_v_s, new_slc_k_p, new_slc_k_s, new_slc_v_p, new_slc_v_s,
     new_conv_p, new_conv_s) = stacked
    y_prompt = _rms_norm(xp, norm_final)
    y_sample = _rms_norm(xs, norm_final)
    return (y_prompt, y_sample, new_a_k_p, new_a_k_s, new_a_v_p, new_a_v_s, new_win_k_p, new_win_k_s,
            new_win_v_p, new_win_v_s, new_cmp_k_p, new_cmp_k_s, new_cmp_v_p, new_cmp_v_s, new_slc_k_p,
            new_slc_k_s, new_slc_v_p, new_slc_v_s, new_conv_p, new_conv_s)


_drawn_inputs = setup_inputs


def setup_inputs(seed=0):
    import zlib

    import numpy as np

    out = dict(_drawn_inputs(seed))
    spreads = {}
    factors = {'cache_slc_k': 3.156,
     'norm_attn': 2.807,
     'norm_ffn': 2.84,
     'conv_b': 3.816,
     'norm_final': 3.086}
    for name, (base, spread) in spreads.items():
        noise = np.random.default_rng([zlib.crc32(name.encode()), seed]).standard_normal(out[name].shape)
        drawn = base * np.exp(spread * noise) if base else spread * noise
        out[name] = jnp.asarray(drawn.astype(out[name].dtype))
    for name, factor in factors.items():
        out[name] = (out[name] * factor).astype(out[name].dtype)
    return out
```

```python
from contextlib import ExitStack

import numpy as np
import concourse.bass as bass
from concourse import mybir

F32 = mybir.dt.float32
I32 = mybir.dt.int32
ALU = mybir.AluOpType
ACT = mybir.ActivationFunctionType
AXX = mybir.AxisListType.X

P = 128
D = 1024
KC = D // P
SEQ = 1024
NB, NT = 8, 4
RS = NB * NT
ROWS = SEQ + RS
NTILE = SEQ // P + 1
HD = 64
HA = HB = 8
PAST = 8192
PAGE = 128
NPAGE = PAST // PAGE
POOL = NB * NPAGE * 5 // 4
LA = 2048
LW = 512
DFF = 2816
NFF = DFF // P
EPS = 1e-6
NEG = -1e30
SCALE = HD ** -0.5
TOP = PAST + NT - 1
SLEN = 8704
A0, AW = 6144, 2560
W0, WW = 7168, 1536


def rows_of(t):
    return P if t < SEQ // P else RS


class Mem:

    def __init__(self, nc, stack, stage):
        self.nc, self.stack, self.stage, self.sems = nc, stack, stage, []
        stack.callback(self.end)

    def sb(self, name, shape, dt=F32):
        return self.stack.enter_context(self.nc.sbuf_tensor(f"{self.stage}_{name}", shape, dt))

    def ps(self, name, shape):
        return self.stack.enter_context(self.nc.psum_tensor(f"{self.stage}_{name}", shape, F32))

    def sem(self, name):
        handle = self.nc.alloc_semaphore(name=f"{self.stage}_{name}")
        self.sems.append(handle)
        return handle

    def end(self):
        if self.sems:
            self.nc.clear_and_free_semaphores(self.sems)
            self.nc.all_engine_barrier()

    def block(self):
        return self.stack.enter_context(self.nc.Block())


def move_window(queue, io, scr, cache, new, out, length, first, width, s_moved):
    for b in range(NB):
        queue.dma_start(io[out][b, 0:length - NT, :], io[cache][b, NT:length, :]).then_inc(s_moved, 16)
    queue.dma_start(io[out][:, length - NT:length, :],
                    scr[new][:, first:first + width].rearrange("(b t) c -> b t c", t=NT)).then_inc(s_moved, 16)


def input_projection(nc, io, scr):
    NP = 6
    W_CHUNKS = [(512, 512), (1024, 512), (2048, 512), (2560, 280), (0, 512), (1536, 512)]
    WBUF = 3
    row_groups = [(0, 512), (512, 512), (SEQ, RS)]

    jobs = []
    for t in range(NTILE):
        jobs += [("x", t, 0), ("x", t, 1)]
    later = []
    for ch in range(4):
        for t in range(NTILE):
            jobs.append(("n", ch, t))
            if ch in (0, 2, 3):
                later.append((len(jobs) - 1, ("k", ch, t)))
            if later and later[0][0] <= len(jobs) - 2:
                src, job = later.pop(0)
                jobs.append((*job, src))
    for ch in (4, 5):
        for c in range(4):
            for rg in range(3):
                jobs.append(("q", ch, c, rg))
                if later:
                    src, job = later.pop(0)
                    jobs.append((*job, src))
    NJ = len(jobs)
    first_use = {ch: min(j for j, x in enumerate(jobs) if x[0] in "nq" and x[1] == ch) for ch in range(6)}
    last_use = {ch: max(j for j, x in enumerate(jobs) if x[0] in "nq" and x[1] == ch) for ch in range(6)}

    def stores(j):
        job = jobs[j]
        out = []
        if job[0] == "n":
            ch, t = job[1], job[2]
            n = rows_of(t)
            if t < 8:
                r = slice(t * P, t * P + n)
                if ch == 0:
                    out.append((io["new_a_k_p"][r, :], n, 0, 512))
                if ch == 1:
                    out.append((io["new_a_v_p"][r, :], n, 0, 512))
                if ch == 2:
                    for i, name in enumerate(("cmp_k", "cmp_v", "slc_k", "slc_v")):
                        out.append((io[f"new_{name}_p"][r, :], n, i * P, P))
                if ch == 3:
                    out.append((scr["vw"][r, :], n, P, P))
                    if t >= 4:
                        r4 = slice(t * P - LW, t * P - LW + n)
                        out.append((io["new_win_k_p"][r4, :], n, 0, P))
                        out.append((io["new_win_v_p"][r4, :], n, P, P))
                    out.append((scr["gates"][r, :], n, 256, 24))
            else:
                if ch == 0:
                    out.append((scr["s_ak"][:, :], n, 0, 512))
                if ch == 1:
                    out.append((scr["s_av"][:, :], n, 0, 512))
                if ch == 2:
                    for i, name in enumerate(("cmp_k", "cmp_v", "slc_k", "slc_v")):
                        out.append((io[f"new_{name}_s"][:, :], n, i * P, P))
                if ch == 3:
                    out.append((scr["s_w"][:, :], n, 0, 256))
                    out.append((scr["gates"][SEQ:ROWS, :], n, 256, 24))
        return out

    def n_stores(j):
        job = jobs[j]
        if job[0] == "x":
            return 0
        if job[0] == "n":
            return len(stores(j))
        if job[0] == "k":
            return 4 if job[1] == 0 else 1
        return 1

    stored, total = [], [0] * NP
    for j in range(NJ):
        total[j % NP] += 16 * n_stores(j)
        stored.append(total[j % NP])

    with ExitStack() as stack:
        m = Mem(nc, stack, "in")
        xin = m.sb("xin", [P, NTILE, D])
        sq = m.sb("sq", [P, 2, D])
        gain = m.sb("gain", [P, D])
        xT = m.sb("xT", [P, KC, ROWS])
        w = m.sb("w", [P, WBUF, KC, 512])
        yout = m.sb("yout", [P, NP, 512])
        ident = m.sb("ident", [P, P])
        ss = m.sb("ss", [P, NTILE])
        ms = m.sb("ms", [P, NTILE])
        rms2 = m.sb("rms2", [P, NTILE])
        rstd = m.sb("rstd", [P, NTILE])
        ps = m.ps("ps", [P, NP, 512])
        s_x = m.sem("x_loaded")
        s_c = m.sem("consts_loaded")
        s_one = m.sem("padding_set")
        s_sq = m.sem("squares_summed")
        s_ms = m.sem("mean_square")
        s_rstd = m.sem("rstd")
        s_xn = m.sem("x_normed")
        s_w = [m.sem(f"w_loaded{i}") for i in range(WBUF)]
        s_pe = m.sem("job_in_psum")
        s_ev = [m.sem("job_out_by_act"), m.sem("job_out_by_dve")]
        s_st = [m.sem(f"stored{i}") for i in range(NP)]
        block = m.block()

        @block.sync
        def _(sp):
            sp.dma_start(xin[:, 0, :], io["x_prompt"][0:P, :]).then_inc(s_x, 16)
            for t in range(1, NTILE):
                src = io["x_prompt"][t * P:t * P + P, :] if t < 8 else io["x_sample"][:, :]
                sp.dma_start(xin[0:rows_of(t), t, :], src).then_inc(s_x, 16)
            sp.dma_start(ident[:, :], io["c_ident"][:, :]).then_inc(s_c, 16)
            sp.dma_start(gain[:, :], io["norm_attn"].partition_broadcast(P)).then_inc(s_c, 16)
            for ch, (c0, n) in enumerate(W_CHUNKS):
                if ch >= WBUF:
                    sp.wait_ge(s_pe, last_use[ch - WBUF] + 1)
                sp.dma_start(w[:, ch % WBUF, :, 0:n],
                             io["w_in"][:, c0:c0 + n].rearrange("(k p) n -> p k n", p=P)).then_inc(s_w[ch % WBUF], 16)

        @block.tensor
        def _(pe):
            pe.wait_ge(s_c, 32)
            for j, job in enumerate(jobs):
                if j >= NP:
                    pe.wait_ge(s_ev[j % 2], (j - NP) // 2 + 1)
                b = j % NP
                if job[0] == "x":
                    _, t, half = job
                    n = rows_of(t)
                    pe.wait_ge(s_xn, t + 1)
                    for k in range(4):
                        kk = half * 4 + k
                        mm = pe.transpose(ps[:, b, k * P:k * P + n], xin[0:n, t, kk * P:kk * P + P], ident[0:n, 0:n])
                elif job[0] == "n":
                    _, ch, t = job
                    n = rows_of(t)
                    width = W_CHUNKS[ch][1]
                    if t == 0:
                        pe.wait_ge(s_w[ch % WBUF], 16 * (ch // WBUF + 1))
                        if ch == 0:
                            pe.wait_ge(s_ev[0], NTILE)
                            pe.wait_ge(s_ev[1], NTILE)
                    for k in range(KC):
                        mm = pe.matmul(ps[0:n, b, 0:width], xT[:, k, t * P:t * P + n], w[:, ch % WBUF, k, 0:width],
                                       start=(k == 0), stop=(k == KC - 1))
                elif job[0] == "k":
                    _, ch, t, src = job
                    n = rows_of(t)
                    pe.wait_ge(s_ev[src % 2], src // 2 + 1)
                    cols = {0: [0, 1, 2, 3], 2: [2], 3: [0]}[ch]
                    for i, c in enumerate(cols):
                        mm = pe.transpose(ps[:, b, i * P:i * P + n], yout[0:n, src % NP, c * P:c * P + P],
                                          ident[0:n, 0:n])
                else:
                    _, ch, c, rg = job
                    r0, n = row_groups[rg]
                    if c == 0 and rg == 0:
                        pe.wait_ge(s_w[ch % WBUF], 16 * (ch // WBUF + 1))
                    for k in range(KC):
                        mm = pe.matmul(ps[:, b, 0:n], w[:, ch % WBUF, k, c * P:c * P + P], xT[:, k, r0:r0 + n],
                                       start=(k == 0), stop=(k == KC - 1))
                mm.then_inc(s_pe, 1)

        def copy_out(eng, j, copy, sigmoid=None):
            job = jobs[j]
            b = j % NP
            eng.wait_ge(s_pe, j + 1)
            if j >= NP and stored[j - NP]:
                eng.wait_ge(s_st[b], stored[j - NP])
            if job[0] == "x":
                _, t, half = job
                n = rows_of(t)
                return copy(xT[:, half * 4:half * 4 + 4, t * P:t * P + n],
                            ps[:, b, :].rearrange("p (k n) -> p k n", k=4)[:, :, 0:n], 1.0)
            if job[0] == "n":
                _, ch, t = job
                n = rows_of(t)
                return copy(yout[0:n, b, 0:W_CHUNKS[ch][1]], ps[0:n, b, 0:W_CHUNKS[ch][1]], 1.0)
            if job[0] == "k":
                n = rows_of(job[2])
                w4 = 4 if job[1] == 0 else 1
                return copy(yout[:, b, :].rearrange("p (k n) -> p k n", k=4)[:, 0:w4, 0:n],
                            ps[:, b, :].rearrange("p (k n) -> p k n", k=4)[:, 0:w4, 0:n], 1.0)
            n = row_groups[job[3]][1]
            return copy(yout[:, b, 0:n], ps[:, b, 0:n], SCALE)

        @block.scalar
        def _(act):
            act.wait_ge(s_one, 1)
            for t in range(NTILE):
                act.wait_ge(s_x, 16 * NTILE)
                if t >= 2:
                    act.wait_ge(s_sq, t - 1)
                n = rows_of(t)
                nc.scalar.activation(sq[0:n, t % 2, :], xin[0:n, t, :], ACT.Square,
                                     accum_out=ss[0:n, t:t + 1]).then_inc(s_sq, 1)
            act.wait_ge(s_ms, 2)
            nc.scalar.activation(rstd[:, :], rms2[:, :], ACT.Sqrt).then_inc(s_rstd, 1)
            for j in range(0, NJ, 2):
                copy_out(act, j, lambda o, i, s: nc.scalar.activation(o, i, ACT.Copy, scale=s)).then_inc(s_ev[0], 1)

        @block.vector
        def _(dve):
            dve.wait_ge(s_sq, NTILE)
            dve.tensor_scalar(ms[:, :], ss[:, :], 1.0 / D, EPS, ALU.mult, ALU.add).then_inc(s_ms, 1)
            dve.wait_ge(s_ms, 1)
            dve.reciprocal(rms2[:, :], ms[:, :]).then_inc(s_ms, 1)
            dve.wait_ge(s_rstd, 1)
            dve.wait_ge(s_c, 32)
            for t in range(NTILE):
                n = rows_of(t)
                dve.scalar_tensor_tensor(out=xin[0:n, t, :], in0=xin[0:n, t, :], scalar=rstd[0:n, t:t + 1],
                                         in1=gain[0:n, :], op0=ALU.mult, op1=ALU.mult).then_inc(s_xn, 1)
            for j in range(1, NJ, 2):
                copy_out(dve, j, lambda o, i, s: dve.tensor_scalar(o, i, s, None, ALU.mult)).then_inc(s_ev[1], 1)

        @block.gpsimd
        def _(pool):
            pool.memset(ss[:, :], 1.0).then_inc(s_one, 1)
            for j, job in enumerate(jobs):
                if job[0] == "x":
                    continue
                b = j % NP
                pool.wait_ge(s_ev[j % 2], j // 2 + 1)
                if job[0] == "n":
                    for dst, n, c0, width in stores(j):
                        pool.dma_start(dst, yout[0:n, b, c0:c0 + width]).then_inc(s_st[b], 16)
                elif job[0] == "k":
                    _, ch, t, src = job
                    n = rows_of(t)
                    h0 = {0: 0, 2: 8, 3: 10}[ch]
                    for i in range(4 if ch == 0 else 1):
                        pool.dma_start(scr["kT"][h0 * HD + i * P:h0 * HD + i * P + P, t * P:t * P + n],
                                       yout[:, b, i * P:i * P + n]).then_inc(s_st[b], 16)
                else:
                    _, ch, c, rg = job
                    r0, n = row_groups[rg]
                    q0 = 0 if ch == 4 else 512
                    pool.dma_start(scr["qT"][q0 + c * P:q0 + c * P + P, r0:r0 + n],
                                   yout[:, b, 0:n]).then_inc(s_st[b], 16)
            for b in range(NP):
                pool.wait_ge(s_st[b], total[b])


def bias_tables(nc, io, scr):
    CH = 512
    NCH = SLEN // CH
    tables = [("tabS", 0, SLEN), ("tabA", A0, AW), ("tabW", W0, WW)]
    H = HA + HB
    with ExitStack() as stack:
        m = Mem(nc, stack, "tab")
        onehot = m.sb("onehot", [32, SLEN])
        rel = m.sb("rel", [32, H])
        add = m.sb("add", [H, SLEN + AW + WW])
        res = m.sb("res", [H, SLEN + AW + WW])
        ps = m.ps("ps", [H, 4, CH])
        s_in = m.sem("loaded")
        s_mm = m.sem("chunk_in_psum")
        s_add = m.sem("chunk_added")
        s_out = m.sem("stored")
        block = m.block()
        adds, n = [], 0
        for c in range(NCH):
            n += sum(o <= c * CH < o + ln for _, o, ln in tables)
            adds.append(n)

        @block.sync
        def _(sp):
            sp.dma_start(rel[:, :], io["rel_bias"][:, :]).then_inc(s_in, 16)
            sp.dma_start(onehot[:, :], io["c_onehot"][:, :]).then_inc(s_in, 16)
            sp.dma_start(add[:, :], io["c_masks"].partition_broadcast(H)).then_inc(s_in, 16)
            sp.wait_ge(s_add, adds[-1])
            at = 0
            for name, _, ln in tables:
                sp.dma_start(scr[name][:, :], res[:, at:at + ln]).then_inc(s_out, 16)
                at += ln
            sp.wait_ge(s_out, 16 * len(tables))

        @block.tensor
        def _(pe):
            pe.wait_ge(s_in, 48)
            for c in range(NCH):
                if c >= 4:
                    pe.wait_ge(s_add, adds[c - 4])
                pe.matmul(ps[:, c % 4, :], rel[:, :], onehot[:, c * CH:c * CH + CH],
                          start=True, stop=True).then_inc(s_mm, 1)

        @block.vector
        def _(dve):
            for c in range(NCH):
                dve.wait_ge(s_mm, c + 1)
                at = 0
                for _, o, ln in tables:
                    if o <= c * CH < o + ln:
                        x = at + c * CH - o
                        dve.tensor_tensor(res[:, x:x + CH], ps[:, c % 4, :], add[:, x:x + CH],
                                          ALU.add).then_inc(s_add, 1)
                    at += ln


def prompt_attention(nc, io, scr, s_moved):
    QT = SEQ // P
    kinds = [
        dict(tab="tabA", tab0=7172 - A0, q0=0, k0=0, share=1, v="new_a_v_p", o0=0, gate=None, back=QT),
        dict(tab="tabS", tab0=7172, q0=8, k0=8, share=4, v="new_slc_v_p", o0=512, gate=1, back=QT),
        dict(tab="tabW", tab0=7172 - W0, q0=8, k0=10, share=4, v="vw", o0=512, gate=2, back=LW // P),
    ]

    def span(kd, qt):
        j0 = max(0, qt - kd["back"])
        return j0, qt + 1 - j0

    with ExitStack() as stack:
        m = Mem(nc, stack, "pa")
        mix = m.sb("mix", [P, QT, D])
        gates = m.sb("gates", [P, QT, 24])
        gsig = m.sb("gsig", [P, QT, 24])
        ident = m.sb("ident", [P, P])
        flip = m.sb("flip", [P, P])
        s_free = m.sem("buffer_free")
        s_c = m.sem("consts_loaded")
        s_gs = m.sem("gates_ready")
        mixT = m.sb("mixT", [P, 2, SEQ])

        for ki, kd in enumerate(kinds):
            units = [(hh, qt) for hh in range(2) for qt in range(QT)]
            NU = len(units)
            banks, n = [], 0
            for _, qt in units:
                n += -(-span(kd, qt)[1] // 4)
                banks.append(n)
            NBK = banks[-1]
            assert NBK % 2 == 0
            with ExitStack() as inner:
                k = Mem(nc, inner, f"pa{ki}")
                qT = k.sb("qT", [P, 2, SEQ])
                kT = k.sb("kT", [P, 2, SEQ])
                s_pad = k.sem("padding_zeroed")
                V = k.sb("V", [P, 2, QT, HD])
                hank = k.sb("hank", [P, 2, SEQ])
                T = k.sb("T", [P, 2, SEQ])
                L = k.sb("L", [P, 3, SEQ])
                Pr = k.sb("Pr", [P, 3, SEQ])
                PT = k.sb("PT", [P, 3, SEQ])
                mx = k.sb("mx", [P, NU])
                nm = k.sb("nm", [P, NU])
                sm = k.sb("sm", [P, NU])
                rg = k.sb("rg", [P, NU])
                rgg = k.sb("rgg", [P, NU])
                psS = k.ps("psS", [P, 2, SEQ])
                psT = k.ps("psT", [P, 2, 512])
                psF = k.ps("psF", [P, 512])
                psO = k.ps("psO", [P, 4, HD])
                s_ld = [k.sem(f"head_loaded{i}") for i in range(2)]
                s_fl = k.sem("bias_flipped")
                s_T = k.sem("bias_copied")
                s_qk = k.sem("scores_in_psum")
                s_mx = k.sem("logits_and_max")
                s_nm = k.sem("max_negated")
                s_ex = k.sem("probs")
                s_tr = k.sem("probs_transposed")
                s_cp = k.sem("probs_t_copied")
                s_pv = k.sem("pv_in_psum")
                s_rg = k.sem("weight_ready")
                s_o = k.sem("unit_added")
                block = k.block()

                @block.sync
                def _(sp):
                    if ki == 0:
                        sp.dma_start(ident[:, :], io["c_ident"][:, :]).then_inc(s_c, 16)
                        sp.dma_start(flip[:, :], io["c_flip"][:, :]).then_inc(s_c, 16)
                        sp.dma_start(gates[:, :, :], scr["gates"][0:SEQ, :].rearrange("(t p) n -> p t n", p=P)).then_inc(s_c, 16)
                        sp.dma_start(mix[:, :, 512:], scr["mixc"].rearrange("(t p) n -> p t n", p=P)).then_inc(s_c, 16)
                    vsrc = (scr if kd["v"] in scr else io)[kd["v"]].rearrange("(t p) n -> p t n", p=P)
                    tab = scr[kd["tab"]]
                    width = tab.shape[1]

                    def load(i, hh):
                        h = i * 2 + hh
                        kv = h // kd["share"]
                        sp.dma_start(qT[0:HD, hh, :], scr["qT"][bass.ds(kd["q0"] * HD + h * HD, HD), 0:SEQ]).then_inc(s_ld[hh], 16)
                        sp.dma_start(kT[0:HD, hh, :], scr["kT"][bass.ds(kv * HD + kd["k0"] * HD, HD), 0:SEQ]).then_inc(s_ld[hh], 16)
                        src = bass.AP(tab.tensor, h * width + (kd["q0"] * width + kd["tab0"]), [[1, P], [1, SEQ]])
                        sp.dma_start(hank[:, hh, :], src).then_inc(s_ld[hh], 16)
                        sp.dma_start(V[:, hh, :, :], vsrc[:, :, bass.ds(kv * HD, HD)]).then_inc(s_ld[hh], 16)

                    load(0, 0)
                    load(0, 1)
                    with sp.Fori(1, 4) as i:
                        sp.wait_ge(s_o, i * NU - QT)
                        load(i, 0)
                        sp.wait_ge(s_o, i * NU)
                        load(i, 1)

                @block.gpsimd
                def _(pool):
                    pool.memset(qT[HD:P, :, :], 0.0).then_inc(s_pad, 1)
                    pool.memset(kT[HD:P, :, :], 0.0).then_inc(s_pad, 1)

                @block.tensor
                def _(pe):
                    if ki == 0:
                        pe.wait_ge(s_c, 64)
                    pe.wait_ge(s_pad, 2)

                    def flip_bias(i, hh):
                        for half in range(2):
                            n = 2 * hh + half
                            pe.wait_ge(s_T, i * 4 + n)
                            pe.matmul(psF[:, :], flip[:, :], hank[:, hh, half * 512:half * 512 + 512],
                                      start=True, stop=True).then_inc(s_fl, 1)

                    def scores(i, u):
                        hh, qt = units[u]
                        pe.wait_ge(s_mx, i * NU + max(0, u - 1))
                        j0, nk = span(kd, qt)
                        for c in range(0, nk * P, 512):
                            w = min(512, nk * P - c)
                            mm = pe.matmul(psS[:, u % 2, c:c + w], qT[:, hh, qt * P:qt * P + P],
                                           kT[:, hh, j0 * P + c:j0 * P + c + w], start=True, stop=True)
                        mm.then_inc(s_qk, 1)

                    def transposes(i, u):
                        hh, qt = units[u]
                        nk = span(kd, qt)[1]
                        pe.wait_ge(s_ex, i * NU + u + 1)
                        c = banks[u - 1] if u else 0
                        for j in range(0, nk, 4):
                            if c >= 2:
                                pe.wait_ge(s_cp, i * NBK + c - 1)
                            for jj in range(j, min(j + 4, nk)):
                                mm = pe.transpose(psT[:, c % 2, (jj - j) * P:(jj - j) * P + P],
                                                  Pr[:, u % 3, jj * P:jj * P + P], ident[:, :])
                            mm.then_inc(s_tr, 1)
                            c += 1

                    def values(i, u):
                        hh, qt = units[u]
                        j0, nk = span(kd, qt)
                        pe.wait_ge(s_cp, i * NBK + banks[u])
                        pe.wait_ge(s_o, i * NU + u)
                        for j in range(nk):
                            mm = pe.matmul(psO[:, u % 4, :], PT[:, u % 3, j * P:j * P + P], V[:, hh, j0 + j, :],
                                           start=(j == 0), stop=(j == nk - 1))
                        mm.then_inc(s_pv, 1)

                    with pe.Fori(0, 4) as i:
                        for u in range(NU + 3):
                            if u in (0, QT // 2):
                                pe.wait_ge(s_ld[2 * u // QT], i * 64 + 64)
                            if u < NU:
                                scores(i, u)
                            if 2 <= u < NU + 2:
                                transposes(i, u - 2)
                            if u >= 3:
                                values(i, u - 3)
                            if u in (0, QT // 2):
                                flip_bias(i, 2 * u // QT)

                @block.scalar
                def _(act):
                    if ki == 0:
                        move_window(act, io, scr, "cache_a_k", "s_ak", "new_a_k_s", LA, 0, 512, s_moved)
                        act.wait_ge(s_c, 64)
                        nc.scalar.activation(gsig[:, :, :], gates[:, :, :], ACT.Sigmoid).then_inc(s_gs, 1)
                    with act.Fori(0, 4) as i:
                        for u in range(NU + 2):
                            if u >= 2:
                                v = u - 2
                                nk = span(kd, units[v][1])[1]
                                c = banks[v - 1] if v else 0
                                if v == 0 or v >= 3:
                                    act.wait_ge(s_pv, i * NU + max(0, v - 2))
                                for j in range(0, nk, 4):
                                    w = min(4, nk - j) * P
                                    act.wait_ge(s_tr, i * NBK + c + 1)
                                    nc.scalar.activation(PT[:, v % 3, j * P:j * P + w], psT[:, c % 2, 0:w],
                                                         ACT.Copy).then_inc(s_cp, 1)
                                    c += 1
                            if u < NU:
                                w = span(kd, units[u][1])[1] * P
                                act.wait_ge(s_nm, i * NU + u + 1)
                                if u >= 3:
                                    act.wait_ge(s_tr, i * NBK + banks[u - 3])
                                nc.scalar.activation(Pr[:, u % 3, 0:w], L[:, u % 3, 0:w], ACT.Exp,
                                                     bias=nm[:, u:u + 1], scale=1.0,
                                                     accum_out=sm[:, u:u + 1]).then_inc(s_ex, 1)

                @block.vector
                def _(dve):
                    if ki == 0:
                        dve.wait_ge(s_c, 64)
                        dve.memset(mix[:, :, 0:512], 0.0).then_inc(s_gs, 1)
                        dve.wait_ge(s_gs, 2)

                    def bias_copies(i, hh):
                        for half in range(2):
                            dve.wait_ge(s_fl, i * 4 + 2 * hh + half + 1)
                            dve.tensor_copy(T[:, hh, half * 512:half * 512 + 512], psF[:, :]).then_inc(s_T, 1)

                    def logits(i, u):
                        hh, qt = units[u]
                        j0, nk = span(kd, qt)
                        w = nk * P
                        if u % QT == 0:
                            dve.wait_ge(s_T, i * 4 + 2 * hh + 2)
                        dve.wait_ge(s_qk, i * NU + u + 1)
                        if u >= 3:
                            dve.wait_ge(s_ex, i * NU + u - 2)
                        dve.sem_inc(s_free, 1)
                        dve.tensor_tensor_reduce(L[:, u % 3, 0:w], psS[:, u % 2, 0:w], T[:, hh, SEQ - w:SEQ],
                                                 1.0, NEG, ALU.add, ALU.max, mx[:, u:u + 1]).then_inc(s_mx, 1)
                        dve.wait_ge(s_mx, i * NU + u + 1)
                        dve.tensor_scalar(nm[:, u:u + 1], mx[:, u:u + 1], -1.0, None, ALU.mult).then_inc(s_nm, 1)

                    def finish(i, u):
                        hh, qt = units[u]
                        dve.wait_ge(s_ex, i * NU + u + 1)
                        dve.reciprocal(rg[:, u:u + 1], sm[:, u:u + 1]).then_inc(s_rg, 1)
                        per = 1
                        weight = rg
                        if kd["gate"] is not None:
                            per = 2
                            dve.wait_ge(s_rg, i * NU * 2 + 2 * u + 1)
                            dve.tensor_tensor(rgg[:, u:u + 1], rg[:, u:u + 1],
                                              gsig[:, qt, bass.ds(i * 6 + (3 * hh + kd["gate"]), 1)],
                                              ALU.mult).then_inc(s_rg, 1)
                            weight = rgg
                        dve.wait_ge(s_rg, i * NU * per + per * (u + 1))
                        dve.wait_ge(s_pv, i * NU + u + 1)
                        o = mix[:, qt, bass.ds(i * 2 * HD + (kd["o0"] + hh * HD), HD)]
                        dve.scalar_tensor_tensor(out=o, in0=psO[:, u % 4, :], scalar=weight[:, u:u + 1], in1=o,
                                                 op0=ALU.mult, op1=ALU.add).then_inc(s_o, 1)

                    with dve.Fori(0, 4) as i:
                        bias_copies(i, 0)
                        for u in range(NU + 3):
                            if u < NU:
                                logits(i, u)
                            if u == QT // 2:
                                bias_copies(i, 1)
                            if u >= 3:
                                finish(i, u - 3)

        with ExitStack() as inner:
            k = Mem(nc, inner, "paT")
            psM = k.ps("psM", [P, 4, 512])
            s_m = k.sem("mix_transposed")
            s_mc = k.sem("mix_copied")
            s_ms = [k.sem(f"mix_stored{i}") for i in range(2)]
            block = k.block()

            @block.tensor
            def _(pe):
                for c in range(2 * KC):
                    if c >= 4:
                        pe.wait_ge(s_mc, c - 3)
                    for t in range(4):
                        tt = (c % 2) * 4 + t
                        mm = pe.transpose(psM[:, c % 4, t * P:t * P + P], mix[:, tt, (c // 2) * P:(c // 2) * P + P],
                                          ident[:, :])
                    mm.then_inc(s_m, 1)

            @block.vector
            def _(dve):
                for c in range(2 * KC):
                    dve.wait_ge(s_m, c + 1)
                    if c // 2 >= 2:
                        dve.wait_ge(s_ms[(c // 2) % 2], 16 * (c // 4))
                    dve.tensor_copy(mixT[:, (c // 2) % 2, (c % 2) * 512:(c % 2) * 512 + 512],
                                    psM[:, c % 4, :]).then_inc(s_mc, 1)

            @block.sync
            def _(sp):
                for c in range(KC):
                    sp.wait_ge(s_mc, 2 * c + 2)
                    sp.dma_start(scr["mixT"][c * P:c * P + P, 0:SEQ], mixT[:, c % 2, :]).then_inc(s_ms[c % 2], 16)
                for i in range(2):
                    sp.wait_ge(s_ms[i], 16 * KC // 2)


def compress(nc, io, scr, idx):
    NQ = 4
    TQ = HD // NQ
    PB = SEQ // HD
    with ExitStack() as stack:
        m = Mem(nc, stack, "cmp")
        ident = m.sb("ident", [P, P])
        ptr = m.sb("ptr", [P, NB], I32)
        odd = m.sb("odd", [P, NQ], I32)
        idx4 = m.sb("idx4", [P, NB], I32)
        cur = m.sb("cur", [P, NQ], I32)
        w1 = m.sb("w1", [P, 2, HD, P])
        w2 = m.sb("w2", [P, 2, P])
        raw = m.sb("raw", [P, 2 * NQ, TQ, P])
        KT = m.sb("KT", [P, 2, TQ, P])
        bias = m.sb("bias", [P, 2])
        hid = m.sb("hid", [P, 2, P])
        kv_out = m.sb("kv_out", [P, 2, P])
        psT = m.ps("psT", [P, 4, 512])
        psH = m.ps("psH", [P, 2, 512])
        psK = m.ps("psK", [P, 2, P])
        s_free = m.sem("buffer_free")
        s_z = m.sem("zeroed")
        s_c = m.sem("consts_loaded")
        s_i = m.sem("indices_ready")
        s_cur = m.sem("turns_indices_ready")
        s_w = m.sem("weights_loaded")
        s_pp = m.sem("prompt_blocks_loaded")
        s_ld = [m.sem(f"chunk_loaded{c}") for c in range(2 * NQ)]
        s_tb = m.sem("bank_transposed")
        s_ev = [m.sem("bank_copied_by_act"), m.sem("bank_copied_by_dve")]
        s_mm = m.sem("chunk_multiplied")
        s_b = m.sem("bias_copied")
        s_g = m.sem("gelu_done")
        s_2 = m.sem("compressed_in_psum")
        s_o = m.sem("compressed_copied")
        s_st = m.sem("compressed_stored")
        block = m.block()
        caches = [io[n].rearrange("(n x) p c -> n (x p c)", x=1).rearrange("n (q e) -> (n q) e", q=2 * NQ)
                  for n in ("cache_cmp_k", "cache_cmp_v")]
        NC = 2 * NQ

        @block.sync
        def _(sp):
            sp.dma_start(ident[:, :], io["c_ident"][:, :]).then_inc(s_c, 16)
            sp.dma_start(odd[:, :], io["c_odd"][:, :]).then_inc(s_c, 16)
            for b in range(NB):
                src = bass.AP(io["page_table"].tensor, b * NPAGE, [[1, NPAGE], [0, 2], [1, 1]])
                sp.dma_start(ptr[:, b:b + 1], src, allow_slow_non_contiguous=True).then_inc(s_c, 16)
            for kv, n in enumerate("kv"):
                new = io[f"new_cmp_{n}_p"].rearrange("(b t) c -> b t c", t=HD)
                for q in range(NQ):
                    c = kv * NQ + q
                    sp.dma_start(raw[0:PB, c, :, :], new[:, q * TQ:q * TQ + TQ, :]).then_inc(s_pp, 16)
                    for g in range(2):
                        sp.dma_start(raw[PB:PB + 1, c, :, g * HD:g * HD + HD],
                                     io[f"pe_cmp_{n}"][q * TQ:q * TQ + TQ, :].unsqueeze(0)).then_inc(s_pp, 16)
            sp.wait_ge(s_z, 2)
            for kv, n in enumerate("kv"):
                for g in range(2):
                    r = slice(g * HD, g * HD + HD)
                    sp.dma_start(w1[r, kv, :, r], io[f"w_cmp_{n}1"].rearrange("(t d) o -> d t o", d=HD)).then_inc(s_w, 16)
                    sp.dma_start(w2[r, kv, r], io[f"w_cmp_{n}2"][:, :]).then_inc(s_w, 16)
            sp.wait_ge(s_o, 2)
            sp.dma_start(scr["kcp"][:, :], kv_out[:, 0, 0:PB]).then_inc(s_st, 16)
            sp.dma_start(scr["vcp"][:, :], kv_out[0:PB, 1, :]).then_inc(s_st, 16)
            with sp.Fori(0, NB) as b:
                sp.wait_ge(s_o, b * 2 + 4)
                sp.dma_start(scr["kcs"][bass.ds(b, 1), :, :].rearrange("n p c -> p n c"),
                             kv_out[:, 0:1, :]).then_inc(s_st, 16)
                sp.dma_start(scr["vcs"][bass.ds(b, 1), :, :].rearrange("n p c -> p n c"),
                             kv_out[:, 1:2, :]).then_inc(s_st, 16)
            sp.wait_ge(s_st, 32 * (NB + 1))

        @block.gpsimd
        def _(pool):
            pool.memset(w1[:, :, :, :], 0.0).then_inc(s_z, 1)
            pool.memset(w2[:, :, :], 0.0).then_inc(s_z, 1)
            pool.wait_ge(s_i, 2)
            with pool.Fori(0, NB) as b:
                for c in range(NC):
                    pool.wait_ge(s_ld[c], b * 16)
                pool.tensor_copy(cur[:, :], idx[:, :, bass.ds(b, 1)].rearrange("p q n -> p (q n)")).then_inc(s_cur, 1)
                pool.wait_ge(s_cur, b + 1)
                for c in range(NC):
                    pool.wait_ge(s_tb, (b * NC + c + 1) * 4)
                    pool.sem_inc(s_free, 1)
                    pool.indirect_dma_start(
                        raw[:, c, :, :].rearrange("p t c -> p (t c)"), None, caches[c // NQ],
                        bass.IndirectOffsetOnAxis(ap=cur[:, c % NQ:c % NQ + 1], axis=0)).then_inc(s_ld[c], 16)

        @block.tensor
        def _(pe):
            pe.wait_ge(s_c, 16 * (2 + NB))
            pe.wait_ge(s_pp, 16 * 3 * NC)

            def transposes(turn, c, n):
                for j in range(4):
                    if not (isinstance(turn, int) and turn == 0 and c == 0):
                        pe.wait_ge(s_ev[j % 2], (turn * NC + c) * 2 - 1 + j // 2)
                    for t in range(TQ // 4):
                        mm = pe.transpose(psT[:, j, t * P:t * P + n], raw[0:n, c, j * (TQ // 4) + t, :], ident[0:n, 0:n])
                    mm.then_inc(s_tb, 1)

            def multiply(turn, c, n):
                kv, q = c // NQ, c % NQ
                if q == 0:
                    if not (isinstance(turn, int) and turn == 0):
                        pe.wait_ge(s_g, turn * 2 + kv - 1)
                pe.wait_ge(s_ev[0], (turn * NC + c + 1) * 2)
                pe.wait_ge(s_ev[1], (turn * NC + c + 1) * 2)
                for t in range(TQ):
                    mm = pe.matmul(psH[:, kv, 0:n], w1[:, kv, q * TQ + t, :], KT[:, c % 2, t, 0:n],
                                   start=(q == 0 and t == 0), stop=(q == NQ - 1 and t == TQ - 1))
                mm.then_inc(s_mm, 1)

            def second(turn, kv, n):
                pe.wait_ge(s_g, turn * 2 + kv + 1)
                pe.wait_ge(s_o, turn * 2 + kv)
                if kv == 0:
                    pe.matmul(psK[:, 0, 0:n], w2[:, 0, :], hid[:, 0, 0:n], start=True, stop=True).then_inc(s_2, 1)
                else:
                    pe.matmul(psK[0:n, 1, :], hid[:, 1, 0:n], w2[:, 1, :], start=True, stop=True).then_inc(s_2, 1)

            def turn_of(turn, n, n2):
                for c in range(NC + 1):
                    if c < NC:
                        if n == P:
                            pe.wait_ge(s_ld[c], 16 * turn)
                        transposes(turn, c, n)
                    if c >= 1:
                        if n < P and c == 1:
                            pe.wait_ge(s_w, 16 * 8)
                        multiply(turn, c - 1, n)
                    if c == NQ + 1:
                        second(turn, 0, n2)
                second(turn, 1, n2)

            turn_of(0, PB + 1, PB)
            with pe.Fori(1, NB + 1) as turn:
                turn_of(turn, P, P)

        def copies(eng, turn, n, which, copy):
            for c in range(NC):
                for j in (which, which + 2):
                    eng.wait_ge(s_tb, (turn * NC + c) * 4 + j + 1)
                    if c >= 2 or not (isinstance(turn, int) and turn == 0):
                        eng.wait_ge(s_mm, turn * NC + c - 1)
                    copy(KT[:, c % 2, j * 4:j * 4 + 4, 0:n],
                         psT[:, j, :].rearrange("p (t n) -> p t n", t=4)[:, :, 0:n]).then_inc(s_ev[which], 1)
                if c == NQ + 1:
                    yield 0
            yield 1

        @block.scalar
        def _(act):
            def turn_of(turn, n, n2):
                for kv in copies(act, turn, n, 0, lambda o, i: nc.scalar.activation(o, i, ACT.Copy)):
                    act.wait_ge(s_mm, turn * NC + NQ * (kv + 1))
                    if n < P:
                        act.wait_ge(s_b, kv + 1)
                    act.wait_ge(s_2, turn * 2 + kv - 1 if kv else turn * 2)
                    nc.scalar.activation(hid[:, kv, 0:n2], psH[:, kv, 0:n2], ACT.Gelu_apprx_tanh,
                                         bias=bias[:, kv:kv + 1], scale=1.0).then_inc(s_g, 1)

            turn_of(0, PB + 1, PB)
            with act.Fori(1, NB + 1) as turn:
                turn_of(turn, P, P)

        @block.vector
        def _(dve):
            dve.wait_ge(s_c, 16 * (2 + NB))
            dve.tensor_scalar(idx4[:, :], ptr[:, :], 2 * NQ, None, ALU.mult).then_inc(s_i, 1)
            dve.wait_ge(s_i, 1)
            for q in range(NQ):
                r = dve.tensor_tensor(idx[:, q, :], idx4[:, :], odd[:, q:q + 1].to_broadcast([P, NB]), ALU.add)
            r.then_inc(s_i, 1)

            def turn_of(turn, n, n2):
                for kv in copies(dve, turn, n, 1, lambda o, i: dve.tensor_copy(o, i)):
                    if n < P:
                        dve.wait_ge(s_mm, NQ * (kv + 1))
                        dve.tensor_copy(bias[:, kv:kv + 1], psH[:, kv, PB:PB + 1]).then_inc(s_b, 1)
                    dve.wait_ge(s_2, turn * 2 + kv + 1)
                    dve.wait_ge(s_st, turn * 32)
                    if n < P and kv == 1:
                        dve.tensor_copy(kv_out[0:n2, kv, :], psK[0:n2, kv, :]).then_inc(s_o, 1)
                    else:
                        dve.tensor_copy(kv_out[:, kv, 0:n2], psK[:, kv, 0:n2]).then_inc(s_o, 1)

            turn_of(0, PB + 1, PB)
            with dve.Fori(1, NB + 1) as turn:
                turn_of(turn, P, P)


def compressed_attention(nc, io, scr, mixB, GB, Qb):
    QT = SEQ // P
    NBLK = PAST // HD
    NR = NB * NT * 2
    with ExitStack() as stack:
        m = Mem(nc, stack, "ca")
        ident = m.sb("ident", [P, P])
        flip = m.sb("flip", [P, P])
        rsum = m.sb("rsum", [P, 2, NR])
        ones = m.sb("ones", [1, P])
        kcs = m.sb("kcs", [P, NB, P])
        vcs = m.sb("vcs", [P, NB, P])
        qs = m.sb("qs", [P, 4, RS])
        biasC = m.sb("biasC", [P, NBLK])
        Ls = m.sb("Ls", [P, 2, NBLK])
        Ps = m.sb("Ps", [P, 2, NBLK])
        Pn = m.sb("Pn", [P, 2, NBLK])
        mxs = m.sb("mxs", [P, 2])
        nms = m.sb("nms", [P, 2])
        sms = m.sb("sms", [P, 2])
        rcs = m.sb("rcs", [P, 2])
        PTs = m.sb("PTs", [P, 2, P])
        score = [m.sb(f"score{i}", [NR, NBLK + 1]) for i in range(3)]
        top8 = m.sb("top8", [NR, 2, 8])
        pen = m.sb("pen", [NR, NBLK])
        penT = m.sb("penT", [P, NR])
        graw = m.sb("graw", [1, 2, RS * 24 // 2])
        qp = m.sb("qp", [P, 4, SEQ])
        kbd = m.sb("kbd", [P, 2, 32])
        vbd = m.sb("vbd", [P, 512])
        hank = m.sb("hank", [P, HB, 16])
        TB = m.sb("TB", [P, HB, 16])
        graws = m.sb("graws", [P, QT, 24])
        gsig = m.sb("gsig", [P, QT, 24])
        Lp = m.sb("Lp", [P, 2, HB, 16])
        Pp = m.sb("Pp", [P, 2, HB, 16])
        PTp = m.sb("PTp", [P, 2, P])
        mxp = m.sb("mxp", [P, QT, HB])
        mcp = m.sb("mcp", [P, QT, HB])
        smp = m.sb("smp", [P, QT, HB])
        sm1 = m.sb("sm1", [P, QT, HB])
        rcp = m.sb("rcp", [P, QT, HB])
        rgp = m.sb("rgp", [P, QT, HB])
        outp = m.sb("outp", [P, 2, 512])
        psB = m.ps("psB", [P, 512])
        psC = m.ps("psC", [P, 2, 512])
        psD = m.ps("psD", [P, 512])
        psE = m.ps("psE", [P, 2, 512])
        psG = m.ps("psG", [P, 512])
        s_c = m.sem("loaded")
        s_z = m.sem("zeroed")
        s_q = m.sem("queries_spread")
        s_p = m.sem("prompt_operands")
        s_pe = m.sem("pe")
        s_v = m.sem("dve")
        s_a = m.sem("act")
        s_po = m.sem("prompt_scores")
        s_pt = m.sem("prompt_probs_transposed")
        s_pv = m.sem("prompt_out_in_psum")
        s_L = m.sem("prompt_logits")
        s_d = m.sem("prompt_softmax_step")
        s_e = m.sem("prompt_exp")
        s_cp = m.sem("prompt_transposed_copied")
        s_o = m.sem("prompt_out")
        s_st = [m.sem(f"prompt_stored{i}") for i in range(2)]
        s_out = m.sem("choice_stored")
        block = m.block()

        @block.gpsimd
        def _(pool):
            pool.memset(Qb[:, :, :, :, :], 0.0).then_inc(s_z, 1)
            pool.memset(kbd[:, :, :], 0.0).then_inc(s_z, 1)
            pool.memset(vbd[:, :], 0.0).then_inc(s_z, 1)
            pool.memset(Pp[:, :, :, :], 0.0).then_inc(s_z, 1)
            pool.memset(ones[:, :], 1.0).then_inc(s_z, 1)
            pool.wait_ge(s_z, 5)
            for g in range(2):
                for half in range(2):
                    pool.dma_start(kbd[half * HD:half * HD + HD, g, half * 16:half * 16 + 16],
                                   scr["kcp"][g * HD:g * HD + HD, :]).then_inc(s_p, 16)
            for h in range(HB):
                pool.dma_start(vbd[h * 16:h * 16 + 16, h * HD:h * HD + HD], scr["vcp"][:, h // 4 * HD:h // 4 * HD + HD]).then_inc(s_p, 16)

        @block.sync
        def _(sp):
            sp.dma_start(ident[:, :], io["c_ident"][:, :]).then_inc(s_c, 16)
            sp.dma_start(flip[:, :], io["c_flip"][:, :]).then_inc(s_c, 16)
            sp.dma_start(rsum[:, :, :], io["c_rsum"].rearrange("t p n -> p t n")).then_inc(s_c, 16)
            sp.dma_start(kcs[:, :, :], scr["kcs"].rearrange("n p c -> p n c")).then_inc(s_c, 16)
            sp.dma_start(vcs[:, :, :], scr["vcs"].rearrange("n p c -> p n c")).then_inc(s_c, 16)
            for g in range(2):
                sp.dma_start(qs[g * HD:g * HD + HD, :, :],
                             scr["qT"][512 + g * 256:768 + g * 256, SEQ:ROWS].rearrange("(r d) n -> d r n", d=HD)).then_inc(s_c, 16)
            tab = scr["tabS"]
            for r in range(4):
                for g in range(2):
                    for t in range(NT):
                        row = r * 8 + g * 4 + t
                        src = bass.AP(tab.tensor, (HA + g * 4 + r) * SLEN + 66 - t, [[0, 4], [HD, NBLK], [1, 1]])
                        sp.dma_start(biasC[row:P:32, :].unsqueeze(2), src,
                                     allow_slow_non_contiguous=True).then_inc(s_c, 16)
            sp.wait_ge(s_v, 18)
            sp.dma_start(scr["penT"][:, :], penT[:, :]).then_inc(s_out, 16)
            for qt in range(QT):
                sp.wait_ge(s_o, qt + 1)
                sp.dma_start(scr["mixc"][qt * P:qt * P + P, :], outp[:, qt % 2, :]).then_inc(s_st[qt % 2], 16)
            sp.wait_ge(s_out, 16)
            for i in range(2):
                sp.wait_ge(s_st[i], 16 * QT // 2)

        LOADS = 16 * (7 + 4 * 2 * NT + 1 + 1 + HB + 1)

        @block.tensor
        def _(pe):
            pe.wait_ge(s_c, LOADS)
            pe.wait_ge(s_z, 5)
            pe.wait_ge(s_a, 1)
            for a in range(2):
                mm = pe.matmul(psC[:, a, 0:RS * 24 // 2], ones[:, :], graw[:, a, :], start=True, stop=True)
            mm.then_inc(s_pe, 1)
            pe.wait_ge(s_q, 2)
            for b in range(NB):
                o = 32 * (b % 4)
                mm = pe.matmul(psE[o:o + 32, b // 4, 0:NBLK], Qb[:, b, :, :, :].rearrange("p r g t -> p (r g t)"),
                               kcs[:, b, :], start=True, stop=True, tile_position=(0, o))
            mm.then_inc(s_pe, 1)
            pe.matmul(psG[:, 0:P], flip[:, :], hank[:, :, :].rearrange("p h e -> p (h e)"),
                      start=True, stop=True).then_inc(s_pe, 1)
            pe.wait_ge(s_v, 10)
            for t in range(2):
                mm = pe.matmul(psB[0:NR, 0:NBLK], rsum[:, t, :], Pn[:, t, :], start=(t == 0), stop=(t == 1))
            mm.then_inc(s_pe, 1)
            for t in range(2):
                mm = pe.transpose(psD[:, t * P:t * P + P], Pn[:, t, :], ident[:, :])
            mm.then_inc(s_pe, 1)
            pe.wait_ge(s_a, 4)
            pe.wait_ge(s_v, 3)
            for b in range(NB):
                mm = pe.matmul(psC[:, 0, b * 32:b * 32 + 32], vcs[:, b, :],
                               PTs[:, b // 4, (b % 4) * 32:(b % 4) * 32 + 32], start=True, stop=True)
            mm.then_inc(s_pe, 1)
            pe.wait_ge(s_v, 17)
            pe.transpose(psB[:, 0:NR], pen[:, :], ident[0:NR, 0:NR]).then_inc(s_pe, 1)

            pe.wait_ge(s_p, 16 * 12)
            for qt in range(QT + 1):
                if qt < QT:
                    nb = 2 * qt + 2
                    if qt >= 2:
                        pe.wait_ge(s_L, qt - 1)
                    for c in range(4):
                        mm = pe.matmul(psE[:, qt % 2, c * 32:c * 32 + 32], qp[:, c, qt * P:qt * P + P], kbd[:, c // 2, :],
                                       start=True, stop=True)
                    mm.then_inc(s_po, 1)
                if qt >= 1:
                    v = qt - 1
                    pe.wait_ge(s_e, v + 1)
                    if v >= 1:
                        pe.wait_ge(s_cp, v)
                    pe.transpose(psD[:, 0:P], Pp[:, v % 2, :, :].rearrange("p h b -> p (h b)"), ident[:, :]).then_inc(s_pt, 1)
                    pe.wait_ge(s_cp, v + 1)
                    if v >= 1:
                        pe.wait_ge(s_o, v)
                    pe.matmul(psG[:, :], PTp[:, v % 2, :], vbd[:, :], start=True, stop=True).then_inc(s_pv, 1)

        @block.scalar
        def _(act):
            act.dma_start(graw[:, :, :].rearrange("p a n -> p (a n)"),
                          bass.AP(scr["gates"].tensor, SEQ * 24, [[0, 1], [1, RS * 24]])).then_inc(s_c, 16)
            act.dma_start(qp[:, :, :], scr["qT"][512:1024, 0:SEQ].rearrange("(c p) n -> p c n", p=P)).then_inc(s_c, 16)
            for h in range(HB):
                src = bass.AP(scr["tabS"].tensor, (HA + h) * SLEN + 7235, [[1, P], [HD, 16], [1, 1]])
                act.dma_start(hank[:, h, :].unsqueeze(2), src, allow_slow_non_contiguous=True).then_inc(s_c, 16)
            act.dma_start(graws[:, :, :], scr["gates"][0:SEQ, :].rearrange("(t p) n -> p t n", p=P)).then_inc(s_c, 16)
            act.wait_ge(s_c, LOADS)
            nc.scalar.activation(graw[:, :, :], graw[:, :, :], ACT.Sigmoid).then_inc(s_a, 1)
            nc.scalar.activation(gsig[:, :, :], graws[:, :, :], ACT.Sigmoid).then_inc(s_a, 1)
            act.wait_ge(s_v, 7)
            for t in range(2):
                r = nc.scalar.activation(Ps[:, t, :], Ls[:, t, :], ACT.Exp, bias=nms[:, t:t + 1], scale=1.0,
                                         accum_out=sms[:, t:t + 1])
            r.then_inc(s_a, 1)
            act.wait_ge(s_pe, 5)
            nc.scalar.activation(PTs[:, :, :], psD[:, 0:2 * P].rearrange("p (a n) -> p a n", a=2), ACT.Copy).then_inc(s_a, 1)
            for qt in range(QT):
                nb = 2 * qt + 2
                act.wait_ge(s_d, qt * 6 + 3)
                if qt >= 2:
                    act.wait_ge(s_pt, qt - 1)
                nc.scalar.activation(Pp[:, qt % 2, :, 0:nb], Lp[:, qt % 2, :, 0:nb], ACT.Exp).then_inc(s_e, 1)
                act.wait_ge(s_pt, qt + 1)
                if qt >= 2:
                    act.wait_ge(s_pv, qt - 1)
                nc.scalar.activation(PTp[:, qt % 2, :], psD[:, 0:P], ACT.Copy).then_inc(s_cp, 1)

        @block.vector
        def _(dve):
            dve.wait_ge(s_c, LOADS)
            dve.wait_ge(s_z, 5)
            for g in range(2):
                h = slice(g * HD, g * HD + HD)
                dve.tensor_copy(Qb[h, :, :, g, :], qs[h, :, :].rearrange("p r (b t) -> p b r t", t=NT)).then_inc(s_q, 1)
            dve.wait_ge(s_pe, 1)
            for a in range(2):
                got = psC[:, a, 0:RS * 24 // 2].rearrange("p (b t g n) -> p b g t n", b=4, t=NT, g=2)
                for br in range(3):
                    for r in range(4):
                        put = GB[:, br, a * P:a * P + P].rearrange("p (b r g t) -> p b r g t", b=4, r=4, g=2)
                        last = dve.tensor_copy(put[:, :, r, :, :], got[:, :, :, :, 3 * r + br])
                last.then_inc(s_v, 1)
            dve.wait_ge(s_pe, 3)
            dve.tensor_copy(TB[:, :, :], psG[:, 0:P].rearrange("p (h e) -> p h e", h=HB)).then_inc(s_v, 1)
            for t in range(2):
                r = dve.tensor_tensor(Ls[:, t, :], psE[:, t, 0:NBLK], biasC[:, :], ALU.add)
            r.then_inc(s_v, 1)
            dve.wait_ge(s_v, 4)
            dve.tensor_reduce(mxs[:, :], Ls[:, :, :], AXX, ALU.max).then_inc(s_v, 1)
            dve.wait_ge(s_v, 5)
            for t in range(2):
                dve.tensor_scalar(nms[:, t:t + 1], mxs[:, t:t + 1], -1.0, None, ALU.mult).then_inc(s_v, 1)
            dve.wait_ge(s_a, 3)
            dve.reciprocal(rcs[:, :], sms[:, :]).then_inc(s_v, 1)
            dve.wait_ge(s_v, 8)
            for t in range(2):
                dve.tensor_scalar(Pn[:, t, :], Ps[:, t, :], rcs[:, t:t + 1], None, ALU.mult).then_inc(s_v, 1)
            dve.wait_ge(s_pe, 4)
            dve.tensor_copy(score[0][:, 1:NBLK - 1], psB[0:NR, 1:NBLK - 1]).then_inc(s_v, 1)
            dve.memset(score[0][:, 0:1], 1e4)
            dve.memset(score[0][:, NBLK - 1:NBLK + 1], 1e4).then_inc(s_v, 1)
            for i in range(2):
                dve.wait_ge(s_v, 12 + 2 * i)
                dve.max(top8[:, i, :], score[i][:, :]).then_inc(s_v, 1)
                dve.wait_ge(s_v, 13 + 2 * i)
                dve.match_replace(score[i + 1][:, :], top8[:, i, :], score[i][:, :], -1e9).then_inc(s_v, 1)
            dve.wait_ge(s_v, 16)
            dve.tensor_scalar(pen[:, :], score[2][:, 0:NBLK], -1e8, NEG, ALU.is_gt, ALU.mult).then_inc(s_v, 1)
            dve.wait_ge(s_pe, 7)
            dve.tensor_copy(penT[:, :], psB[:, 0:NR]).then_inc(s_v, 1)
            dve.tensor_tensor(mixB[:, :], psC[:, 0, 0:256], GB[:, 0, :], ALU.mult).then_inc(s_v, 1)
            dve.wait_ge(s_a, 2)

            def finish(v):
                dve.wait_ge(s_pv, v + 1)
                if v >= 2:
                    dve.wait_ge(s_st[v % 2], 16 * (v // 2))
                dve.tensor_tensor(outp[:, v % 2, :].rearrange("p (h d) -> p h d", h=HB),
                                  psG[:, :].rearrange("p (h d) -> p h d", h=HB),
                                  rgp[:, v, :].unsqueeze(2).to_broadcast([P, HB, HD]), ALU.mult).then_inc(s_o, 1)

            for qt in range(QT):
                nb = 2 * qt + 2
                n = qt * 6
                dve.wait_ge(s_po, qt + 1)
                if qt >= 2:
                    dve.wait_ge(s_e, qt - 1)
                L = Lp[:, qt % 2, :, 0:nb]
                dve.tensor_tensor(L, psE[:, qt % 2, 0:P].rearrange("p (h b) -> p h b", h=HB)[:, :, 0:nb],
                                  TB[:, :, 16 - nb:16], ALU.add).then_inc(s_L, 1)
                dve.wait_ge(s_L, qt + 1)
                dve.tensor_reduce(mxp[:, qt, :], L, AXX, ALU.max).then_inc(s_d, 1)
                dve.wait_ge(s_d, n + 1)
                dve.tensor_scalar(mcp[:, qt, :], mxp[:, qt, :], NEG / 10, None, ALU.max).then_inc(s_d, 1)
                dve.wait_ge(s_d, n + 2)
                dve.tensor_tensor(L, L, mcp[:, qt, :].unsqueeze(2).to_broadcast([P, HB, nb]), ALU.subtract).then_inc(s_d, 1)
                if qt >= 1:
                    finish(qt - 1)
                dve.wait_ge(s_e, qt + 1)
                dve.tensor_reduce(smp[:, qt, :], Pp[:, qt % 2, :, 0:nb], AXX, ALU.add).then_inc(s_d, 1)
                dve.wait_ge(s_d, n + 4)
                dve.tensor_scalar(sm1[:, qt, :], smp[:, qt, :], 0.5, None, ALU.max).then_inc(s_d, 1)
                dve.wait_ge(s_d, n + 5)
                dve.reciprocal(rcp[:, qt, :], sm1[:, qt, :]).then_inc(s_d, 1)
                dve.wait_ge(s_d, n + 6)
                dve.tensor_tensor(rgp[:, qt, :], rcp[:, qt, :], gsig[:, qt, 0:24:3], ALU.mult).then_inc(s_a, 1)
                dve.wait_ge(s_a, 5 + qt)
            finish(QT - 1)
def sample_dilated(nc, io, scr):
    NTL = 8
    FAR = (LA - 512) // 512
    with ExitStack() as stack:
        m = Mem(nc, stack, "sa")
        ident = m.sb("ident", [P, P])
        ones = m.sb("ones", [P, P])
        qs = m.sb("qs", [P, 4, RS])
        Qa = m.sb("Qa", [P, NB, 4, 2, NT])
        stage = m.sb("stage", [NTL, HA, NT, P])
        AB = m.sb("AB", [P, NTL, 32])
        K = [m.sb(f"K{a}", [P, NTL, 512]) for a in range(2)]
        V = [m.sb(f"V{a}", [P, NTL, 512]) for a in range(2)]
        KT = m.sb("KT", [P, 2, 4, P])
        L = m.sb("L", [P, 2, NTL, 32])
        L2 = m.sb("L2", [P, 2, NTL, 32])
        PA = m.sb("PA", [P, 2, NTL, 32])
        mx = m.sb("mx", [P, 2, 32])
        M = m.sb("M", [P, 2, 32])
        sm = m.sb("sm", [P, 2, 32])
        rc = m.sb("rc", [P, 2, 32])
        mixA = m.sb("mixA", [P, NB, 4, 8])
        psT = m.ps("psT", [P, 2, 512])
        psS = m.ps("psS", [P, 2, 512])
        psO = m.ps("psO", [P, 2, 512])
        psB = m.ps("psB", [P, 512])
        s_free = m.sem("buffer_free")
        s_z = m.sem("zeroed")
        s_c = m.sem("consts_loaded")
        s_q = m.sem("queries_spread")
        s_bt = m.sem("bias_transposed")
        s_bc = m.sem("bias_copied")
        s_ld = [m.sem(f"sequence_loaded{a}") for a in range(2)]
        s_tr = m.sem("keys_transposed")
        s_kc = m.sem("keys_t_copied")
        s_qk = m.sem("scores_in_psum")
        s_qt = m.sem("tile_scored")
        s_L = m.sem("logits")
        s_mx = m.sem("max_of_partition")
        s_M = m.sem("max_of_all")
        s_sub = m.sem("max_subtracted")
        s_ex = m.sem("probs")
        s_sm = m.sem("sum_of_partition")
        s_pv = m.sem("out_in_psum")
        s_rc = m.sem("reciprocal")
        s_o = m.sem("sequence_out")
        s_st = m.sem("stored")
        block = m.block()
        PER = 2 * (FAR + 2)

        @block.sync
        def _(sp):
            sp.dma_start(ident[:, :], io["c_ident"][:, :]).then_inc(s_c, 16)
            sp.dma_start(qs[:, :, :], scr["qT"][0:512, SEQ:ROWS].rearrange("(c p) n -> p c n", p=P)).then_inc(s_c, 16)
            tab = scr["tabA"].tensor
            for t in range(NT):
                for h in range(HA):
                    sp.dma_start(stage[0:FAR, h, t, :].rearrange("p (m f) -> p m f", f=4),
                                 bass.AP(tab, h * AW + 3 - t, [[512, FAR], [16, 32], [1, 4]])).then_inc(s_c, 16)
                sp.dma_start(stage[FAR:NTL, :, t, :],
                             bass.AP(tab, 3 - t + LA - 512, [[P, NTL - FAR], [AW, HA], [1, P]])).then_inc(s_c, 16)
            sp.wait_ge(s_z, 5)
            with sp.Fori(0, NB // 2) as i:
                for a in range(2):
                    b = i * 2 + a
                    sp.wait_ge(s_pv, i * 2)
                    for X, name, new in ((K, "cache_a_k", "s_ak"), (V, "cache_a_v", "s_av")):
                        cache = io[name]
                        for tl in range(FAR):
                            src = cache[bass.ds(b, 1), 512 * tl:512 * tl + 512, :].rearrange(
                                "n (m x) c -> (n m) x c", x=16)[:, 0:4, :]
                            sp.dma_start(X[a][:, tl, :], src).then_inc(s_ld[a], 16)
                        sp.dma_start(X[a][:, FAR:NTL - 1, :],
                                     cache[bass.ds(b, 1), LA - 512:LA, :].rearrange("n (t p) c -> (n p) t c", p=P)).then_inc(s_ld[a], 16)
                        sp.dma_start(X[a][0:NT, NTL - 1, :], scr[new][bass.ds(b * NT, NT), :]).then_inc(s_ld[a], 16)
            sp.wait_ge(s_o, NB)
            for c in range(4):
                for h2 in range(2):
                    r = slice(h2 * HD, h2 * HD + HD)
                    sp.dma_start(scr["mixT"][c * P + h2 * HD:c * P + h2 * HD + HD, SEQ:ROWS].rearrange("p (b t) -> p b t", t=NT),
                                 mixA[r, :, c, h2 * NT:h2 * NT + NT]).then_inc(s_st, 16)
            sp.wait_ge(s_st, 16 * 8)

        @block.gpsimd
        def _(pool):
            for a in range(2):
                pool.memset(K[a][:, NTL - 1, :], 0.0).then_inc(s_z, 1)
                pool.memset(V[a][:, NTL - 1, :], 0.0).then_inc(s_z, 1)
            pool.memset(Qa[:, :, :, :, :], 0.0).then_inc(s_z, 1)
            pool.memset(ones[:, :], 1.0).then_inc(s_z, 1)
            with pool.Fori(0, NB // 2) as i:
                for a in range(2):
                    pool.wait_ge(s_mx, i * 2 + a + 1)
                    pool.wait_ge(s_sub, i * 2)
                    pool.sem_inc(s_free, 1)
                    nc.gpsimd.partition_all_reduce(M[:, a, :], mx[:, a, :], P, bass.bass_isa.ReduceOp.max).then_inc(s_M, 1)

        @block.tensor
        def _(pe):
            pe.wait_ge(s_c, 16 * (2 + NT * (HA + 1)))
            pe.wait_ge(s_z, 6)
            for h in range(HA):
                for t in range(NT):
                    o = (h * NT + t) * NTL
                    mm = pe.transpose(psB[:, o:o + NTL], stage[:, h, t, :], ident[0:NTL, 0:NTL])
            mm.then_inc(s_bt, 1)
            pe.wait_ge(s_q, 2)

            with pe.Fori(0, NB // 2) as i:
                for a in range(2):
                    n = i * 2 + a
                    pe.wait_ge(s_ld[a], (i + 1) * 16 * PER)
                    for tl in range(NTL + 1):
                        if tl < NTL:
                            if tl >= 2:
                                pe.wait_ge(s_kc, n * NTL + tl - 1)
                            for c in range(4):
                                mm = pe.transpose(psT[:, tl % 2, c * P:c * P + P], K[a][:, tl, c * P:c * P + P], ident[:, :])
                            mm.then_inc(s_tr, 1)
                        if tl >= 1:
                            v = tl - 1
                            if v == 0:
                                pe.wait_ge(s_L, i * 2)
                            pe.wait_ge(s_kc, n * NTL + v + 1)
                            for c in range(4):
                                mm = pe.matmul(psS[:, a, v * 32 + c * 8:v * 32 + c * 8 + 8], KT[:, v % 2, c, :],
                                               Qa[:, bass.ds(n, 1), c, :, :].rearrange("p b h t -> p (b h t)"),
                                               start=True, stop=True)
                            if v == NTL - 1:
                                mm.then_inc(s_qk, 1)
                            else:
                                mm.then_inc(s_qt, 1)
                for a in range(2):
                    n = i * 2 + a
                    pe.wait_ge(s_ex, n + 1)
                    pe.wait_ge(s_o, i * 2)
                    for c in range(4):
                        for tl in range(NTL):
                            pe.matmul(psO[:, a, c * 8:c * 8 + 8], V[a][:, tl, c * P:c * P + P],
                                      PA[:, a, tl, c * 8:c * 8 + 8], start=(tl == 0), stop=(tl == NTL - 1))
                    pe.wait_ge(s_sm, n + 1)
                    pe.matmul(psO[:, a, 32:64], ones[:, :], sm[:, a, :], start=True, stop=True).then_inc(s_pv, 1)

        @block.scalar
        def _(act):
            with act.Fori(0, NB // 2) as i:
                for a in range(2):
                    n = i * 2 + a
                    for tl in range(NTL):
                        act.wait_ge(s_tr, n * NTL + tl + 1)
                        if tl >= 2:
                            act.wait_ge(s_qt, n * (NTL - 1) + tl - 1)
                        elif tl == 0:
                            act.wait_ge(s_qk, n)
                        nc.scalar.activation(KT[:, tl % 2, :, :], psT[:, tl % 2, :].rearrange("p (c n) -> p c n", c=4),
                                             ACT.Copy).then_inc(s_kc, 1)
                for a in range(2):
                    n = i * 2 + a
                    act.wait_ge(s_sub, n + 1)
                    act.wait_ge(s_pv, i * 2)
                    nc.scalar.activation(PA[:, a, :, :], L2[:, a, :, :], ACT.Exp).then_inc(s_ex, 1)

        @block.vector
        def _(dve):
            dve.wait_ge(s_c, 16 * (2 + NT * (HA + 1)))
            dve.wait_ge(s_z, 5)
            for h2 in range(2):
                r = slice(h2 * HD, h2 * HD + HD)
                dve.tensor_copy(Qa[r, :, :, h2, :], qs[r, :, :].rearrange("p c (b t) -> p b c t", t=NT)).then_inc(s_q, 1)
            dve.wait_ge(s_bt, 1)
            dve.tensor_copy(AB[:, :, :], psB[:, 0:32 * NTL].rearrange("p (c n) -> p n c", n=NTL)).then_inc(s_bc, 1)
            dve.wait_ge(s_bc, 1)
            with dve.Fori(0, NB // 2) as i:
                for a in range(2):
                    n = i * 2 + a
                    dve.wait_ge(s_qk, n + 1)
                    dve.tensor_tensor(L[:, a, :, :], psS[:, a, 0:32 * NTL].rearrange("p (n c) -> p n c", c=32),
                                      AB[:, :, :], ALU.add).then_inc(s_L, 1)
                    dve.wait_ge(s_L, n + 1)
                    dve.wait_ge(s_M, i * 2)
                    dve.tensor_reduce(mx[:, a, :], L[:, a, :, :].rearrange("p n c -> p c n"), AXX, ALU.max).then_inc(s_mx, 1)
                for a in range(2):
                    n = i * 2 + a
                    dve.wait_ge(s_M, n + 1)
                    dve.wait_ge(s_ex, i * 2)
                    dve.tensor_tensor(L2[:, a, :, :], L[:, a, :, :], M[:, a, :].unsqueeze(1).to_broadcast([P, NTL, 32]),
                                      ALU.subtract).then_inc(s_sub, 1)
                for a in range(2):
                    n = i * 2 + a
                    dve.wait_ge(s_ex, n + 1)
                    dve.wait_ge(s_pv, i * 2)
                    dve.tensor_reduce(sm[:, a, :], PA[:, a, :, :].rearrange("p n c -> p c n"), AXX, ALU.add).then_inc(s_sm, 1)
                for a in range(2):
                    n = i * 2 + a
                    dve.wait_ge(s_pv, n + 1)
                    dve.reciprocal(rc[:, a, :], psO[:, a, 32:64]).then_inc(s_rc, 1)
                    dve.wait_ge(s_rc, n + 1)
                    dve.tensor_tensor(mixA[:, bass.ds(n, 1), :, :].rearrange("p b c n -> p (b c n)"), psO[:, a, 0:32],
                                      rc[:, a, :], ALU.mult).then_inc(s_o, 1)


def sample_selected(nc, io, scr, mixB, GB, Qb, idx):
    NQ = 4
    TQ = HD // NQ
    NTL = HD + 1 + LW // P + 1
    NSEL = HD + 1
    NC = 2 * NQ
    with ExitStack() as stack:
        m = Mem(nc, stack, "sb")
        ident = m.sb("ident", [P, P])
        ones = m.sb("ones", [P, P])
        cur = m.sb("cur", [P, 2, NQ], I32)
        stack4 = m.sb("stack4", [P, 32])
        OV = m.sb("OV", [P, 2, P])
        penT = m.sb("penT", [P, NB, 8])
        hist = m.sb("hist", [P, HB, HD + 4])
        stage = m.sb("stage", [P, 8, P + 4])
        SB = m.sb("SB", [P, NTL, 4, 8])
        raw = m.sb("raw", [P, NC, TQ, P])
        ext = m.sb("ext", [P, 2, 2, NTL - HD, P])
        KT = m.sb("KT", [P, 2, 4, P])
        L = m.sb("L", [P, NTL, 32])
        PB = m.sb("PB", [P, NTL, 32])
        mx = m.sb("mx", [P, 2, 32])
        M = m.sb("M", [P, 2, 32])
        sm = m.sb("sm", [P, 2, 32])
        rc = m.sb("rc", [P, 2, 32])
        rg = m.sb("rg", [P, 2, 32])
        o1 = m.sb("o1", [P, 2, 32])
        psT = m.ps("psT", [P, 3, 512])
        psS = m.ps("psS", [P, 2, 512])
        psO = m.ps("psO", [P, 512])
        psV = m.ps("psV", [P, 2, P])
        s_ov = m.sem("values_copied")
        s_free = m.sem("buffer_free")
        s_z = m.sem("zeroed")
        s_c = m.sem("consts_loaded")
        s_bt = m.sem("bias_transposed")
        s_bc = m.sem("bias_copied")
        s_cur = [m.sem(f"turns_indices_ready_{kv}") for kv in "kv"]
        s_ld = [m.sem(f"chunk_loaded{c}") for c in range(NC)]
        s_le = [m.sem(f"window_loaded{a}") for a in range(2)]
        s_tr = m.sem("keys_transposed")
        s_kc = m.sem("keys_t_copied")
        s_qk = m.sem("scores_in_psum")
        s_L = m.sem("logits")
        s_L2 = m.sem("choice_masked")
        s_mx = m.sem("max_of_partition")
        s_M = m.sem("max_of_all")
        s_sub = m.sem("max_subtracted")
        s_ex = m.sem("probs")
        s_sm = m.sem("sum_of_partition")
        s_pv = m.sem("values_multiplied")
        s_rc = m.sem("weights_ready")
        s_o = m.sem("sequence_out")
        s_st = m.sem("stored")
        block = m.block()
        caches = [io[n].rearrange("(n x) p c -> n (x p c)", x=1).rearrange("n (q e) -> (n q) e", q=2 * NQ)
                  for n in ("cache_slc_k", "cache_slc_v")]
        NTURN = 3
        NBK = -(-NTL // 4)
        NGR = -(-NTL // 16)
        group_tiles = [min(16, NTL - 16 * g) for g in range(NGR)]

        @block.sync
        def _(sp):
            sp.dma_start(ident[:, :], io["c_ident"][:, :]).then_inc(s_c, 16)
            sp.dma_start(penT[:, :, :], scr["penT"].rearrange("p (b n) -> p b n", b=NB)).then_inc(s_c, 16)
            sp.dma_start(hist[:, :, :], bass.AP(scr["tabS"].tensor, HA * SLEN, [[HD, P], [SLEN, HB], [1, HD + 4]])).then_inc(s_c, 16)
            sp.dma_start(stage[0:1, :, :], bass.AP(scr["tabS"].tensor, HA * SLEN + PAST, [[0, 1], [SLEN, HB], [1, P + 4]])).then_inc(s_c, 16)
            sp.dma_start(stage[1:6, :, :], bass.AP(scr["tabW"].tensor, HA * WW + PAST - LW - W0, [[P, 5], [WW, HB], [1, P + 4]])).then_inc(s_c, 16)
            sp.wait_ge(s_z, 1)
            with sp.Fori(0, NB // 2) as i:
                for a in range(2):
                    b = i * 2 + a
                    sp.wait_ge(s_pv, i * 2 * NTURN)
                    for kv, n in enumerate("kv"):
                        sp.dma_start(ext[0:NT, a, kv, 0, :], io[f"new_slc_{n}_s"][bass.ds(b * NT, NT), :]).then_inc(s_le[a], 16)
                        sp.dma_start(ext[:, a, kv, 1:5, :],
                                     io[f"cache_win_{n}"][bass.ds(b, 1), :, :].rearrange("n (t p) c -> (n p) t c", p=P)).then_inc(s_le[a], 16)
                        sp.dma_start(ext[0:NT, a, kv, 5, :], scr["s_w"][bass.ds(b * NT, NT), kv * P:kv * P + P]).then_inc(s_le[a], 16)
            sp.wait_ge(s_o, 2 * NB)
            mix = mixB[:, :].rearrange("p (b r g t) -> p b r g t", b=NB, r=4, g=2)
            for g in range(2):
                for r in range(4):
                    row = 512 + (g * 4 + r) * HD
                    sp.dma_start(scr["mixT"][row:row + HD, SEQ:ROWS].rearrange("p (b t) -> p b t", t=NT),
                                 mix[g * HD:g * HD + HD, :, r, g, :]).then_inc(s_st, 16)
            sp.wait_ge(s_st, 16 * 8)

        @block.gpsimd
        def _(pool):
            pool.memset(ext[:, :, :, :, :], 0.0).then_inc(s_z, 1)
            pool.memset(ones[:, :], 1.0).then_inc(s_z, 1)

            def indices(kv, b):
                for c in range(NQ):
                    pool.wait_ge(s_ld[kv * NQ + c], b * 16)
                pool.tensor_copy(cur[:, kv, :], idx[:, :, bass.ds(b, 1)].rearrange("p q n -> p (q n)")).then_inc(s_cur[kv], 1)
                pool.wait_ge(s_cur[kv], b + 1)

            def gather(kv, c):
                pool.sem_inc(s_free, 1)
                pool.indirect_dma_start(
                    raw[:, kv * NQ + c, :, :].rearrange("p t c -> p (t c)"), None, caches[kv],
                    bass.IndirectOffsetOnAxis(ap=cur[:, kv, c:c + 1], axis=0)).then_inc(s_ld[kv * NQ + c], 16)

            def values(b):
                indices(1, b)
                pool.wait_ge(s_pv, b * NTURN)
                for c in range(NQ):
                    gather(1, c)

            def maximum(b):
                pool.wait_ge(s_mx, b * 2 + 2)
                pool.wait_ge(s_sub, b * 2)
                pool.sem_inc(s_free, 1)
                nc.gpsimd.partition_all_reduce(M[:, :, :], mx[:, :, :], P, bass.bass_isa.ReduceOp.max).then_inc(s_M, 1)

            indices(0, 0)
            for c in range(NQ):
                gather(0, c)
            with pool.Fori(0, NB - 1) as b:
                values(b)
                indices(0, b + 1)
                for c in range(NQ):
                    pool.wait_ge(s_tr, b * NBK + (c + 1) * (TQ // 4))
                    gather(0, c)
                maximum(b)
            values(NB - 1)
            maximum(NB - 1)

        @block.tensor
        def _(pe):
            pe.wait_ge(s_c, 16 * 5)
            pe.wait_ge(s_z, 2)
            for k in range(8):
                for t in range(NT):
                    o = (k * NT + t) * 6
                    mm = pe.transpose(psT[:, 0, o:o + 6], stage[0:6, k, 3 - t:3 - t + P], ident[0:6, 0:6])
            mm.then_inc(s_bt, 1)
            pe.wait_ge(s_bc, 6)

            def turn(b, i, a):
                for k in range(NBK + 1):
                    if k < NBK:
                        t0, n = 4 * k, min(4, NTL - 4 * k)
                        if k % (TQ // 4) == 0 and k < HD // 4:
                            pe.wait_ge(s_ld[k // (TQ // 4)], (b + 1) * 16)
                        if k == HD // 4:
                            pe.wait_ge(s_le[a], (i + 1) * 16 * 6)
                        if k >= 3:
                            pe.wait_ge(s_kc, b * NBK + k - 2)
                        for j in range(n):
                            tl = t0 + j
                            src = raw[:, tl // TQ, tl % TQ, :] if tl < HD else ext[:, a, 0, tl - HD, :]
                            mm = pe.transpose(psT[:, k % 3, j * P:j * P + P], src, ident[:, :])
                        mm.then_inc(s_tr, 1)
                    if k >= 1:
                        v = k - 1
                        t0, n = 4 * v, min(4, NTL - 4 * v)
                        pe.wait_ge(s_kc, b * NBK + v + 1)
                        gr = v // 4
                        if v % 4 == 0:
                            pe.wait_ge(s_L, b * NGR + gr - 1 if gr else b * NGR)
                        for j in range(n):
                            o = ((v % 4) * 4 + j) * 32
                            mm = pe.matmul(psS[:, gr % 2, o:o + 32], KT[:, v % 2, j, :],
                                           Qb[:, bass.ds(b, 1), :, :, :].rearrange("p b r g t -> p (b r g t)"),
                                           start=True, stop=True)
                        mm.then_inc(s_qk, 1)
                pe.wait_ge(s_ex, b + 1)
                pe.wait_ge(s_ov, b)
                for tl in range(NTL):
                    if tl < HD and tl % TQ == 0:
                        pe.wait_ge(s_ld[NQ + tl // TQ], (b + 1) * 16)
                    src = raw[:, NQ + tl // TQ, tl % TQ, :] if tl < HD else ext[:, a, 1, tl - HD, :]
                    w, k, n = (0, tl, NSEL) if tl < NSEL else (1, tl - NSEL, NTL - NSEL)
                    o = 32 * (k % 4)
                    mm = pe.matmul(psV[o:o + 32, w, :], PB[:, tl, :], src, start=(k < 4), stop=(k >= n - 4),
                                   tile_position=(0, o))
                mm.then_inc(s_pv, 1)
                pe.wait_ge(s_sm, b * 2 + 2)
                pe.wait_ge(s_o, b * 2)
                pe.matmul(psO[:, 64:128], ones[:, :], sm[:, :, :].rearrange("p w n -> p (w n)"),
                          start=True, stop=True).then_inc(s_pv, 1)
                pe.wait_ge(s_ov, b + 1)
                for w in range(2):
                    mm = pe.matmul(psO[:, w * 32:w * 32 + 32], OV[:, w, :], stack4[:, :], start=True, stop=True)
                mm.then_inc(s_pv, 1)

            with pe.Fori(0, NB // 2) as i:
                for a in range(2):
                    turn(i * 2 + a, i, a)

        @block.scalar
        def _(act):
            with act.Fori(0, NB) as b:
                for k in range(NBK):
                    n = min(4, NTL - 4 * k)
                    act.wait_ge(s_tr, b * NBK + k + 1)
                    act.wait_ge(s_qk, b * NBK + k - 1 if k else b * NBK)
                    nc.scalar.activation(KT[:, k % 2, 0:n, :], psT[:, k % 3, 0:n * P].rearrange("p (c n) -> p c n", c=n),
                                         ACT.Copy).then_inc(s_kc, 1)
                act.wait_ge(s_sub, b * 2 + 2)
                act.wait_ge(s_pv, b * NTURN)
                act.wait_ge(s_sm, b * 2)
                nc.scalar.activation(PB[:, :, :], L[:, :, :], ACT.Exp).then_inc(s_ex, 1)
                act.wait_ge(s_pv, b * NTURN + 1)
                nc.scalar.activation(OV[:, :, :], psV[:, :, :], ACT.Copy).then_inc(s_ov, 1)

        @block.vector
        def _(dve):
            dve.wait_ge(s_c, 16 * 5)
            for t in range(NT):
                x = hist[:, :, 3 - t:3 - t + HD].rearrange("p (g r) x -> p x r g", g=2)
                for g in range(2):
                    r = dve.tensor_copy(SB[:, 0:HD, :, g * NT + t], x[:, :, :, g])
                r.then_inc(s_bc, 1)
            dve.tensor_reduce(stack4[:, :], ident[:, :].rearrange("p (j n) -> p n j", j=4), AXX, ALU.add).then_inc(s_bc, 1)
            dve.wait_ge(s_bt, 1)
            for g in range(2):
                r = dve.tensor_copy(SB[:, HD:NTL, :, g * NT:g * NT + NT].rearrange("p n r t -> p r t n"),
                                    psT[:, 0, g * 96:g * 96 + 96].rearrange("p (r t n) -> p r t n", r=4, t=NT))
            r.then_inc(s_bc, 1)
            dve.wait_ge(s_bc, 6)
            with dve.Fori(0, NB) as b:
                for g in range(NGR):
                    n = group_tiles[g]
                    last = min(4 * g + 4, NBK)
                    dve.wait_ge(s_qk, b * NBK + last)
                    if g == 0:
                        dve.wait_ge(s_ex, b)
                    o = L[:, 16 * g:16 * g + n, :]
                    dve.tensor_tensor(o, psS[:, g % 2, 0:n * 32].rearrange("p (n c) -> p n c", c=32),
                                      SB[:, 16 * g:16 * g + n, :, :].rearrange("p n r c -> p n (r c)"), ALU.add).then_inc(s_L, 1)
                    if g < NGR - 1:
                        dve.wait_ge(s_L, b * NGR + g + 1)
                        oo = o.rearrange("p n (r c) -> p (n r) c", r=4)
                        dve.tensor_tensor(oo, oo, penT[:, bass.ds(b, 1), :].to_broadcast([P, 64, 8]), ALU.add).then_inc(s_L2, 1)
                dve.wait_ge(s_L, b * NGR + NGR)
                dve.wait_ge(s_L2, b * (NGR - 1) + NGR - 1)
                dve.wait_ge(s_M, b)
                for w, (t0, t1) in enumerate(((0, NSEL), (NSEL, NTL))):
                    dve.tensor_reduce(mx[:, w, :], L[:, t0:t1, :].rearrange("p n c -> p c n"), AXX, ALU.max).then_inc(s_mx, 1)
                dve.wait_ge(s_M, b + 1)
                for w, (t0, t1) in enumerate(((0, NSEL), (NSEL, NTL))):
                    dve.tensor_tensor(L[:, t0:t1, :], L[:, t0:t1, :],
                                      M[:, w:w + 1, :].to_broadcast([P, t1 - t0, 32]), ALU.subtract).then_inc(s_sub, 1)
                dve.wait_ge(s_ex, b + 1)
                dve.wait_ge(s_pv, b * NTURN)
                for w, (t0, t1) in enumerate(((0, NSEL), (NSEL, NTL))):
                    dve.tensor_reduce(sm[:, w, :], PB[:, t0:t1, :].rearrange("p n c -> p c n"), AXX, ALU.add).then_inc(s_sm, 1)
                dve.wait_ge(s_pv, b * NTURN + NTURN)
                dve.reciprocal(rc[:, :, :], psO[:, 64:128].rearrange("p (w n) -> p w n", w=2)).then_inc(s_rc, 1)
                dve.wait_ge(s_rc, b * 3 + 1)
                dve.tensor_tensor(rg[:, :, :], rc[:, :, :], GB[:, 1:3, bass.ds(b * 32, 32)], ALU.mult).then_inc(s_rc, 1)
                dve.wait_ge(s_rc, b * 3 + 2)
                dve.tensor_tensor(o1[:, :, :], psO[:, 0:64].rearrange("p (w n) -> p w n", w=2), rg[:, :, :], ALU.mult).then_inc(s_rc, 1)
                dve.wait_ge(s_rc, b * 3 + 3)
                for w in range(2):
                    dve.tensor_tensor(mixB[:, bass.ds(b * 32, 32)], mixB[:, bass.ds(b * 32, 32)], o1[:, w, :], ALU.add).then_inc(s_o, 1)
                    dve.wait_ge(s_o, b * 2 + w + 1)


def output_projection(nc, io, scr, hT, convT, G):
    NU = 2 * NFF
    NCV = 2 * NB + 4
    with ExitStack() as stack:
        m = Mem(nc, stack, "op")
        ident = m.sb("ident", [P, P])
        gain = m.sb("gain", [P, D])
        space = G[:, :, :].rearrange("p a b -> p (a b)")
        mixT = space[:, 0:KC * ROWS].rearrange("p (k n) -> p k n", k=KC)
        wo = space[:, KC * ROWS:KC * (ROWS + D)].rearrange("p (k n) -> p k n", k=KC)
        cv = space[0:NCV, KC * (ROWS + D):KC * (ROWS + D) + 2 * DFF]
        xin = m.sb("xin", [P, 3, D])
        x1 = m.sb("x1", [P, NTILE, D])
        sq = m.sb("sq", [P, D])
        ss = m.sb("ss", [P, NTILE])
        ms = m.sb("ms", [P, NTILE])
        rms2 = m.sb("rms2", [P, NTILE])
        rstd = m.sb("rstd", [P, NTILE])
        ps = m.ps("ps", [P, 6, 512])
        psC = m.ps("psC", [P, 2, 512])
        s_c = m.sem("consts_loaded")
        s_one = m.sem("padding_set")
        s_w = m.sem("weights_loaded")
        s_x = [m.sem(f"x_loaded{i}") for i in range(3)]
        s_cv = m.sem("conv_transposed")
        s_cc = m.sem("conv_copied")
        s_pe = m.sem("half_in_psum")
        s_x1 = m.sem("half_added")
        s_sq = m.sem("squares_summed")
        s_ms = m.sem("mean_square")
        s_rstd = m.sem("rstd")
        s_xn = m.sem("x_normed")
        s_tr = m.sem("half_transposed")
        s_ev = [m.sem("half_copied_by_act"), m.sem("half_copied_by_dve")]
        s_st = m.sem("x1_stored")
        block = m.block()

        @block.sync
        def _(sp):
            sp.dma_start(ident[:, :], io["c_ident"][:, :]).then_inc(s_c, 16)
            sp.dma_start(gain[:, :], io["norm_ffn"].partition_broadcast(P)).then_inc(s_c, 16)
            sp.dma_start(cv[0:2 * NB, :], io["state_conv"][:, :]).then_inc(s_c, 16)
            sp.dma_start(cv[2 * NB:2 * NB + 3, :], io["conv_w"][:, :]).then_inc(s_c, 16)
            sp.dma_start(cv[2 * NB + 3:NCV, :], io["conv_b"][:, :]).then_inc(s_c, 16)
            sp.dma_start(mixT[:, :, :], scr["mixT"].rearrange("(k p) n -> p k n", p=P)).then_inc(s_w, 16)
            sp.dma_start(wo[:, :, :], io["w_out"].rearrange("(k p) n -> p k n", p=P)).then_inc(s_w, 16)
            for t in range(NTILE):
                if t >= 3:
                    sp.wait_ge(s_x1, 2 * (t - 2))
                src = io["x_prompt"][t * P:t * P + P, :] if t < 8 else io["x_sample"][:, :]
                sp.dma_start(xin[0:rows_of(t), t % 3, :], src).then_inc(s_x[t % 3], 16)
            for t in range(NTILE):
                sp.wait_ge(s_x1, 2 * t + 2)
                n = rows_of(t)
                sp.dma_start(scr["x1"][t * P:t * P + n, :], x1[0:n, t, :]).then_inc(s_st, 16)
            sp.wait_ge(s_st, 16 * NTILE)

        @block.tensor
        def _(pe):
            pe.wait_ge(s_c, 80)
            for u in range(NU):
                mm = pe.transpose(psC[:, u // NFF, (u % NFF) * NCV:(u % NFF) * NCV + NCV], cv[:, u * P:u * P + P],
                                  ident[0:NCV, 0:NCV])
            mm.then_inc(s_cv, 1)
            pe.wait_ge(s_w, 32)
            for t in range(NTILE):
                n = rows_of(t)
                for half in range(2):
                    j = 2 * t + half
                    if j >= 6:
                        pe.wait_ge(s_x1, j - 5)
                    for k in range(KC):
                        mm = pe.matmul(ps[0:n, j % 6, :], mixT[:, k, t * P:t * P + n], wo[:, k, half * 512:half * 512 + 512],
                                       start=(k == 0), stop=(k == KC - 1))
                    mm.then_inc(s_pe, 1)
            for t in range(NTILE):
                n = rows_of(t)
                for half in range(2):
                    j = 2 * t + half
                    pe.wait_ge(s_xn, t + 1)
                    if j >= 6:
                        pe.wait_ge(s_ev[j % 2], (j - 6) // 2 + 1)
                    else:
                        pe.wait_ge(s_x1, 2 * NTILE)
                    for k in range(4):
                        kk = half * 4 + k
                        mm = pe.transpose(ps[:, j % 6, k * P:k * P + n], x1[0:n, t, kk * P:kk * P + P], ident[0:n, 0:n])
                    mm.then_inc(s_tr, 1)

        def copies(eng, which, copy):
            for t in range(NTILE):
                n = rows_of(t)
                j = 2 * t + which
                eng.wait_ge(s_tr, j + 1)
                copy(hT[:, which * 4:which * 4 + 4, t * P:t * P + n],
                     ps[:, j % 6, :].rearrange("p (k n) -> p k n", k=4)[:, :, 0:n]).then_inc(s_ev[which], 1)

        @block.scalar
        def _(act):
            act.wait_ge(s_one, 1)
            for t in range(NTILE):
                n = rows_of(t)
                act.wait_ge(s_x1, 2 * t + 2)
                if t >= 1:
                    act.wait_ge(s_sq, t)
                nc.scalar.activation(sq[0:n, :], x1[0:n, t, :], ACT.Square, accum_out=ss[0:n, t:t + 1]).then_inc(s_sq, 1)
            act.wait_ge(s_ms, 2)
            nc.scalar.activation(rstd[:, :], rms2[:, :], ACT.Sqrt).then_inc(s_rstd, 1)
            copies(act, 0, lambda o, i: nc.scalar.activation(o, i, ACT.Copy))

        @block.vector
        def _(dve):
            dve.wait_ge(s_cv, 1)
            dve.tensor_copy(convT[:, :, :].rearrange("p (a u) n -> p a (u n)", a=2), psC[:, :, 0:NFF * NCV]).then_inc(s_cc, 1)
            for t in range(NTILE):
                n = rows_of(t)
                dve.wait_ge(s_x[t % 3], 16 * (t // 3 + 1))
                for half in range(2):
                    j = 2 * t + half
                    dve.wait_ge(s_pe, j + 1)
                    c = slice(half * 512, half * 512 + 512)
                    dve.tensor_tensor(x1[0:n, t, c], ps[0:n, j % 6, :], xin[0:n, t % 3, c], ALU.add).then_inc(s_x1, 1)
            dve.wait_ge(s_sq, NTILE)
            dve.tensor_scalar(ms[:, :], ss[:, :], 1.0 / D, EPS, ALU.mult, ALU.add).then_inc(s_ms, 1)
            dve.wait_ge(s_ms, 1)
            dve.reciprocal(rms2[:, :], ms[:, :]).then_inc(s_ms, 1)
            dve.wait_ge(s_rstd, 1)
            dve.wait_ge(s_c, 80)
            for t in range(NTILE):
                n = rows_of(t)
                dve.wait_ge(s_st, 16 * NTILE)
                dve.scalar_tensor_tensor(out=x1[0:n, t, :], in0=x1[0:n, t, :], scalar=rstd[0:n, t:t + 1],
                                         in1=gain[0:n, :], op0=ALU.mult, op1=ALU.mult).then_inc(s_xn, 1)
            copies(dve, 1, lambda o, i: dve.tensor_copy(o, i))

        @block.gpsimd
        def _(pool):
            pool.memset(ss[:, :], 1.0).then_inc(s_one, 1)


def up_projection(nc, io, scr, hT, convT, G, cs, s_moved):
    WBUF = 4
    RG = [(0, 512), (512, 512), (SEQ, RS)]
    with ExitStack() as stack:
        m = Mem(nc, stack, "up")
        w = [m.sb(f"w{i}", [P, 2, KC, P]) for i in range(2)]
        U = m.sb("U", [P, 2, 2, SEQ + 2])
        S = m.sb("S", [P, 2, 2, NB, NT + 2])
        C = m.sb("C", [P, 2, ROWS])
        Z = m.sb("Z", [P, ROWS])
        ps = m.ps("ps", [P, 6, 512])
        s_w = [m.sem(f"weights_loaded{i}") for i in range(2)]
        s_pe = m.sem("group_in_psum")
        s_z = m.sem("edges_set")
        s_u = m.sem("group_copied")
        s_cv = m.sem("convolution_step")
        s_si = m.sem("gate_through_silu")
        s_g = m.sem("gated")
        s_cs = m.sem("state_kept")
        block = m.block()
        wup = io["w_up"].rearrange("(k p) (v n) -> p v k n", p=P, v=2)

        @block.sync
        def _(sp):
            with sp.Fori(0, NFF // 2) as i:
                for a in range(2):
                    sp.wait_ge(s_pe, i * 12)
                    for v in range(2):
                        sp.dma_start(w[a][:, v, :, :], wup[:, v, :, bass.ds(i * 2 * P + a * P, P)]).then_inc(s_w[a], 16)

        @block.tensor
        def _(pe):
            with pe.Fori(0, NFF // 2) as i:
                for a in range(2):
                    pe.wait_ge(s_w[a], (i + 1) * 32)
                    for v in range(2):
                        for g, (r0, n) in enumerate(RG):
                            b = v * 3 + g
                            pe.wait_ge(s_u, i * 12 + a * 6 + b - 5 if a else i * 12)
                            for k in range(KC):
                                mm = pe.matmul(ps[:, b, 0:n], w[a][:, v, k, :], hT[:, k, r0:r0 + n],
                                               start=(k == 0), stop=(k == KC - 1))
                            mm.then_inc(s_pe, 1)

        @block.gpsimd
        def _(pool):
            pool.memset(U[:, :, :, 0:2], 0.0).then_inc(s_z, 1)
            with pool.Fori(0, NFF // 2) as i:
                for a in range(2):
                    j = i * 2 + a
                    pool.wait_ge(s_u, i * 12 + a * 6 + 6)
                    for v in range(2):
                        u = j + v * NFF
                        pool.tensor_copy(cs[:, bass.ds(u, 1), 0:2], U[:, a:a + 1, v, SEQ:SEQ + 2])
                        pool.tensor_copy(cs[:, bass.ds(u, 1), 2:2 + 2 * NB].rearrange("p u (b t) -> p (u b) t", t=2),
                                         S[:, a, v, :, NT:NT + 2]).then_inc(s_cs, 1)

        @block.scalar
        def _(act):
            move_window(act, io, scr, "cache_a_v", "s_av", "new_a_v_s", LA, 0, 512, s_moved)
            move_window(act, io, scr, "cache_win_k", "s_w", "new_win_k_s", LW, 0, P, s_moved)
            move_window(act, io, scr, "cache_win_v", "s_w", "new_win_v_s", LW, P, P, s_moved)
            with act.Fori(0, NFF // 2) as i:
                for a in range(2):
                    j = i * 2 + a
                    act.wait_ge(s_cv, i * 12)
                    act.wait_ge(s_cs, i * 4)
                    for v in range(2):
                        u = j + v * NFF
                        for g, (r0, n) in enumerate(RG):
                            b = v * 3 + g
                            act.wait_ge(s_pe, i * 12 + a * 6 + b + 1)
                            if g < 2:
                                nc.scalar.activation(U[:, a, v, 2 + r0:2 + r0 + n], ps[:, b, 0:n], ACT.Copy).then_inc(s_u, 1)
                            else:
                                nc.scalar.activation(S[:, a, v, :, 0:2],
                                                     convT[:, bass.ds(u, 1), 0:2 * NB].rearrange("p u (b t) -> p (u b) t", t=2), ACT.Copy)
                                nc.scalar.activation(S[:, a, v, :, 2:NT + 2],
                                                     ps[:, b, 0:n].rearrange("p (b t) -> p b t", t=NT), ACT.Copy).then_inc(s_u, 1)
                    act.wait_ge(s_cv, i * 12 + a * 6 + 6)
                    act.wait_ge(s_g, i * 2 + a)
                    nc.scalar.activation(Z[:, :], C[:, 0, :], ACT.Silu).then_inc(s_si, 1)

        @block.vector
        def _(dve):
            dve.wait_ge(s_z, 1)
            with dve.Fori(0, NFF // 2) as i:
                for a in range(2):
                    j = i * 2 + a
                    for v in range(2):
                        u = j + v * NFF
                        n = i * 12 + a * 6 + v * 3
                        dve.wait_ge(s_u, i * 12 + a * 6 + v * 3 + 3)
                        tap = lambda k: convT[:, bass.ds(u, 1), 2 * NB + k:2 * NB + k + 1].rearrange("p u n -> p (u n)")
                        Cs = C[:, v, SEQ:ROWS].rearrange("p (b t) -> p b t", t=NT)
                        dve.wait_ge(s_si, i * 2 + a)
                        dve.wait_ge(s_g, i * 2 + a)
                        dve.tensor_scalar(C[:, v, 0:SEQ], U[:, a, v, 0:SEQ], tap(0), tap(3), ALU.mult, ALU.add)
                        dve.tensor_scalar(Cs, S[:, a, v, :, 0:NT], tap(0), tap(3), ALU.mult, ALU.add).then_inc(s_cv, 1)
                        for k in (1, 2):
                            dve.wait_ge(s_cv, n + k)
                            dve.scalar_tensor_tensor(out=C[:, v, 0:SEQ], in0=U[:, a, v, k:k + SEQ], scalar=tap(k),
                                                     in1=C[:, v, 0:SEQ], op0=ALU.mult, op1=ALU.add)
                            dve.scalar_tensor_tensor(out=Cs, in0=S[:, a, v, :, k:k + NT], scalar=tap(k),
                                                     in1=Cs, op0=ALU.mult, op1=ALU.add).then_inc(s_cv, 1)
                    dve.wait_ge(s_si, i * 2 + a + 1)
                    dve.wait_ge(s_cv, i * 12 + a * 6 + 6)
                    dve.tensor_tensor(G[:, bass.ds(j, 1), :].rearrange("p u n -> p (u n)"), Z[:, :], C[:, 1, :],
                                      ALU.mult).then_inc(s_g, 1)


def down_projection(nc, io, scr, G, cs, s_moved):
    NS = 2 + 2 * NB
    with ExitStack() as stack:
        m = Mem(nc, stack, "dn")
        ident = m.sb("ident", [P, P])
        gain = m.sb("gain", [P, D])
        w = m.sb("w", [P, NFF, D])
        xin = m.sb("xin", [P, 2, 512])
        x2 = m.sb("x2", [P, 2, D])
        sq = m.ps("sq", [P, D])
        tail = m.sb("tail", [NS, 2, 512])
        ss = m.sb("ss", [P, NTILE])
        ms = m.sb("ms", [P, NTILE])
        rms2 = m.sb("rms2", [P, NTILE])
        rstd = m.sb("rstd", [P, NTILE])
        ps = m.ps("ps", [P, 4, 512])
        psC = m.ps("psC", [NS, 2, 512])
        s_c = m.sem("consts_loaded")
        s_w = [m.sem(f"weights_loaded{i}") for i in range(2)]
        s_x = [m.sem(f"x_loaded{i}") for i in range(2)]
        s_tc = m.sem("state_transposed")
        s_tk = m.sem("state_copied")
        s_ts = [m.sem(f"state_stored{i}") for i in range(2)]
        s_pe = m.sem("half_in_psum")
        s_x2 = m.sem("half_added")
        s_sq = m.sem("squares_summed")
        s_ms = m.sem("mean_square")
        s_rstd = m.sem("rstd")
        s_y = m.sem("y_ready")
        s_st = [m.sem(f"y_stored{i}") for i in range(2)]
        block = m.block()
        NTC = 2 * NFF // 4

        def out_tile(sp, t):
            n = rows_of(t)
            sp.wait_ge(s_y, t + 1)
            dst = io["y_prompt"][t * P:t * P + n, :] if t < 8 else io["y_sample"][:, :]
            sp.dma_start(dst, x2[0:n, t % 2, :]).then_inc(s_st[t % 2], 16)

        @block.sync
        def _(sp):
            sp.dma_start(ident[:, :], io["c_ident"][:, :]).then_inc(s_c, 16)
            sp.dma_start(gain[:, :], io["norm_final"].partition_broadcast(P)).then_inc(s_c, 16)
            wd = io["w_down"].rearrange("(j p) n -> p j n", p=P)
            for half in range(2):
                sp.dma_start(w[:, :, half * 512:half * 512 + 512], wd[:, :, half * 512:half * 512 + 512]).then_inc(s_w[half], 16)
            for t in range(NTILE):
                n = rows_of(t)
                for half in range(2):
                    if t >= 1:
                        sp.wait_ge(s_x2, 2 * t + half - 1)
                    sp.dma_start(xin[0:n, half, :], scr["x1"][t * P:t * P + n, half * 512:half * 512 + 512]).then_inc(s_x[half], 16)
                if t >= 1:
                    out_tile(sp, t - 1)
            out_tile(sp, NTILE - 1)
            sp.wait_ge(s_moved, 4 * (NB + 1) * 16)
            for i in range(2):
                sp.wait_ge(s_st[i], 16 * len(range(i, NTILE, 2)))

        @block.gpsimd
        def _(pool):
            for c in range(NTC):
                pool.wait_ge(s_tk, c + 1)
                pool.dma_start(io["new_conv_p"][:, c * 512:c * 512 + 512], tail[0:2, c % 2, :]).then_inc(s_ts[c % 2], 16)
                pool.dma_start(io["new_conv_s"][:, c * 512:c * 512 + 512], tail[2:NS, c % 2, :]).then_inc(s_ts[c % 2], 16)
            for i in range(2):
                pool.wait_ge(s_ts[i], 32 * len(range(i, NTC, 2)))

        @block.tensor
        def _(pe):
            pe.wait_ge(s_c, 32)
            for c in range(NTC):
                if c >= 2:
                    pe.wait_ge(s_tk, c - 1)
                for j in range(4):
                    mm = pe.transpose(psC[:, c % 2, j * P:j * P + P], cs[:, c * 4 + j, :], ident[:, :])
                mm.then_inc(s_tc, 1)
            for t in range(NTILE):
                n = rows_of(t)
                for half in range(2):
                    j = 2 * t + half
                    if t == 0:
                        pe.wait_ge(s_w[half], 16)
                    if j >= 4:
                        pe.wait_ge(s_x2, j - 3)
                    for k in range(NFF):
                        mm = pe.matmul(ps[0:n, j % 4, :], G[:, k, t * P:t * P + n], w[:, k, half * 512:half * 512 + 512],
                                       start=(k == 0), stop=(k == NFF - 1))
                    mm.then_inc(s_pe, 1)

        @block.scalar
        def _(act):
            for c in range(NTC):
                act.wait_ge(s_tc, c + 1)
                if c >= 2:
                    act.wait_ge(s_ts[c % 2], 32 * (c // 2))
                nc.scalar.activation(tail[:, c % 2, :], psC[:, c % 2, :], ACT.Copy).then_inc(s_tk, 1)
            for t in range(NTILE):
                n = rows_of(t)
                act.wait_ge(s_x2, 2 * t + 2)
                if t >= 1:
                    act.wait_ge(s_sq, t)
                nc.scalar.activation(sq[0:n, :], x2[0:n, t % 2, :], ACT.Square, accum_out=ss[0:n, t:t + 1]).then_inc(s_sq, 1)
                act.wait_ge(s_ms, 2 * t + 2)
                nc.scalar.activation(rstd[0:n, t:t + 1], rms2[0:n, t:t + 1], ACT.Sqrt).then_inc(s_rstd, 1)

        @block.vector
        def _(dve):
            dve.wait_ge(s_c, 32)
            for t in range(NTILE):
                n = rows_of(t)
                if t >= 2:
                    dve.wait_ge(s_st[t % 2], 16 * (t // 2))
                for half in range(2):
                    j = 2 * t + half
                    dve.wait_ge(s_x[half], 16 * (t + 1))
                    dve.wait_ge(s_pe, j + 1)
                    c = slice(half * 512, half * 512 + 512)
                    dve.tensor_tensor(x2[0:n, t % 2, c], ps[0:n, j % 4, :], xin[0:n, half, :], ALU.add).then_inc(s_x2, 1)
                dve.wait_ge(s_sq, t + 1)
                dve.tensor_scalar(ms[0:n, t:t + 1], ss[0:n, t:t + 1], 1.0 / D, EPS, ALU.mult, ALU.add).then_inc(s_ms, 1)
                dve.wait_ge(s_ms, 2 * t + 1)
                dve.reciprocal(rms2[0:n, t:t + 1], ms[0:n, t:t + 1]).then_inc(s_ms, 1)
                dve.wait_ge(s_rstd, t + 1)
                dve.scalar_tensor_tensor(out=x2[0:n, t % 2, :], in0=x2[0:n, t % 2, :], scalar=rstd[0:n, t:t + 1],
                                         in1=gain[0:n, :], op0=ALU.mult, op1=ALU.mult).then_inc(s_y, 1)


def hybrid_step(nc, io, scr):
    kernel_stack = ExitStack()
    s_moved = kernel_stack.enter_context(nc.semaphore("windows_moved"))
    bias_tables(nc, io, scr)
    input_projection(nc, io, scr)
    with ExitStack() as stack:
        m = Mem(nc, stack, "sample")
        idx = m.sb("idx", [P, 4, NB], I32)
        Qb = m.sb("Qb", [P, NB, 4, 2, NT])
        mixB = m.sb("mixB", [P, NB * 32])
        GB = m.sb("GB", [P, 3, NB * 32])
        compress(nc, io, scr, idx)
        compressed_attention(nc, io, scr, mixB, GB, Qb)
        sample_selected(nc, io, scr, mixB, GB, Qb, idx)
    sample_dilated(nc, io, scr)
    prompt_attention(nc, io, scr, s_moved)
    with ExitStack() as stack:
        m = Mem(nc, stack, "ffn")
        convT = m.sb("convT", [P, 2 * NFF, 2 * NB + 4])
        cs = m.sb("cs", [P, 2 * NFF, 2 + 2 * NB])
        G = m.sb("G", [P, NFF, ROWS])
        with ExitStack() as inner:
            hT = Mem(nc, inner, "ffnh").sb("hT", [P, KC, ROWS])
            output_projection(nc, io, scr, hT, convT, G)
            up_projection(nc, io, scr, hT, convT, G, cs, s_moved)
        down_projection(nc, io, scr, G, cs, s_moved)
    kernel_stack.close()


def constants():
    dist = TOP - np.arange(SLEN)
    d = np.maximum(dist, 1).astype(np.float32)
    large = 16 + (np.log(d / np.float32(16)) / np.float32(np.log(2048 / 16)) * np.float32(16)).astype(np.int32)
    bucket = np.where(dist < 16, np.maximum(dist, 0), np.minimum(large, 31))
    onehot = (bucket[None, :] == np.arange(32)[:, None]).astype(np.float32)
    full = np.where(dist >= 0, 0.0, NEG)
    groups = (dist <= 128) + 0 + ((dist % 4 == 0) & (dist <= 512)) + ((dist % 16 == 0) & (dist <= LA))
    groups = np.where(dist >= 0, groups, 0)
    counts = np.where(groups > 0, np.log(np.maximum(groups, 1)), NEG)
    window = np.where((dist >= 0) & (dist <= LW), 0.0, NEG)
    masks = np.concatenate([full, counts[A0:A0 + AW], window[W0:W0 + WW]]).astype(np.float32)
    rsum = np.zeros((2, P, 64), np.float32)
    for n in range(2):
        for b in range(4):
            for r in range(4):
                for gt in range(8):
                    rsum[n, b * 32 + r * 8 + gt, (n * 4 + b) * 8 + gt] = 1.0
    odd = (np.arange(P)[:, None] % 2) * 4 + np.arange(4)[None, :]
    return {
        "c_odd": odd.astype(np.int32),
        "c_rsum": rsum,
        "c_onehot": onehot,
        "c_masks": masks,
        "c_ident": np.eye(P, dtype=np.float32),
        "c_flip": np.eye(P, dtype=np.float32)[::-1].copy(),
    }


SCRATCH = {
    "qT": (D, ROWS), "kT": (12 * HD, ROWS), "vw": (SEQ, P), "gates": (ROWS, 24), "s_ak": (RS, 512), "s_av": (RS, 512),
    "s_w": (RS, 2 * P), "tabS": (HA + HB, SLEN), "tabA": (HA + HB, AW), "tabW": (HA + HB, WW), "kcs": (NB, P, P),
    "vcs": (NB, P, P), "kcp": (P, SEQ // HD), "vcp": (SEQ // HD, P), "mixc": (SEQ, 512), "penT": (P, NB * 8),
    "mixT": (D, ROWS), "x1": (ROWS, D),
}
INPUTS = {
    "x_prompt": (SEQ, D), "x_sample": (RS, D), "cache_a_k": (NB, LA, 512), "cache_a_v": (NB, LA, 512),
    "cache_win_k": (NB, LW, P), "cache_win_v": (NB, LW, P), "cache_cmp_k": (POOL, PAGE, P), "cache_cmp_v": (POOL, PAGE, P),
    "cache_slc_k": (POOL, PAGE, P), "cache_slc_v": (POOL, PAGE, P), "state_conv": (2 * NB, 2 * DFF),
    "page_table": (1, NB * NPAGE), "norm_attn": (D,), "w_in": (D, 2840), "rel_bias": (32, HA + HB), "pe_cmp_k": (HD, HD),
    "w_cmp_k1": (HD * HD, HD), "w_cmp_k2": (HD, HD), "pe_cmp_v": (HD, HD), "w_cmp_v1": (HD * HD, HD), "w_cmp_v2": (HD, HD),
    "w_out": (D, D), "norm_ffn": (D,), "w_up": (D, 2 * DFF), "conv_w": (3, 2 * DFF), "conv_b": (1, 2 * DFF),
    "w_down": (DFF, D), "norm_final": (D,),
}
OUTPUTS = {
    "y_prompt": ((SEQ, D), (1, SEQ, D)),
    "y_sample": ((RS, D), (NB, NT, D)),
}
for _n in ("a_k", "a_v"):
    OUTPUTS[f"new_{_n}_p"] = ((SEQ, 512), (1, 1, SEQ, HA, HD))
    OUTPUTS[f"new_{_n}_s"] = ((NB, LA, 512), (1, NB, LA, HA, HD))
for _n in ("win_k", "win_v"):
    OUTPUTS[f"new_{_n}_p"] = ((LW, P), (1, 1, LW, 2, HD))
    OUTPUTS[f"new_{_n}_s"] = ((NB, LW, P), (1, NB, LW, 2, HD))
for _n in ("cmp_k", "cmp_v", "slc_k", "slc_v"):
    OUTPUTS[f"new_{_n}_p"] = ((SEQ, P), (1, 1, SEQ, 2, HD))
    OUTPUTS[f"new_{_n}_s"] = ((RS, P), (1, NB, NT, 2, HD))
OUTPUTS["new_conv_p"] = ((2, 2 * DFF), (1, 1, 2, 2 * DFF))
OUTPUTS["new_conv_s"] = ((2 * NB, 2 * DFF), (1, NB, 2, 2 * DFF))


def kernel(**inputs):
    import concourse.bacc as _bacc
    from concourse.bass_utils import run_bass_kernel_spmd as _run

    nc = _bacc.Bacc("TRN2", target_bir_lowering=False, num_devices=1)
    given = {n: np.asarray(inputs[n]).reshape(s) for n, s in INPUTS.items()} | constants()
    arrays, io = {}, {}
    for name, a in given.items():
        arrays[f"in_{name}"] = np.ascontiguousarray(a)
        io[name] = nc.dram_tensor(f"in_{name}", a.shape, mybir.dt.from_np(a.dtype), kind="ExternalInput").ap()
    for name, (shape, _) in OUTPUTS.items():
        io[name] = nc.dram_tensor(f"out_{name}", shape, F32, kind="ExternalOutput").ap()
    scr = {name: nc.dram_tensor(f"scr_{name}", shape, F32, kind="Internal").ap() for name, shape in SCRATCH.items()}
    hybrid_step(nc, io, scr)
    r = _run(nc, [arrays], core_ids=[0])
    return tuple(np.asarray(r.results[0][f"out_{n}"]).reshape(s) for n, (_, s) in OUTPUTS.items())
```
